# Optimizing a Trainium2 kernel written in Bass

```python
import math
import jax, jax.numpy as jnp
from jax import lax
import numpy as np

D_MODEL = 2048
BATCH = 1
SEQ = 512
DEPTH = 1

CHUNK = 64
D_CONV = 1024
CONV_HEADS = 16
CONV_WIDTH = 3
D_SSM = 1024
SSM_GROUP = 16
SSM_GROUPS = D_SSM // SSM_GROUP
SSM_STATE = 64
D_MIX = D_CONV + D_SSM
N_IN = 4 * D_CONV + 2 * D_SSM
DT_MIN = 1e-3
DT_MAX = 1e-1
EPS = 1e-6

kernel_name = "hybrid_shortconv_s5_block"

def rms_norm(x, g):
    xf = x.astype(jnp.float32)
    y = xf * lax.rsqrt(jnp.mean(xf * xf, axis=-1, keepdims=True) + EPS)
    return (y * g.astype(jnp.float32)).astype(x.dtype)

def causal_dwconv(h, w, b):
    L = h.shape[1]
    hp = jnp.pad(h, ((0, 0), (CONV_WIDTH - 1, 0), (0, 0)))
    out = b[None, None, :]
    for k in range(CONV_WIDTH):
        out = out + w[k][None, None, :] * hp[:, k:k + L, :]
    return out

def _scan_combine(e1, e2):
    a1r, a1i, b1r, b1i = e1
    a2r, a2i, b2r, b2i = e2
    ar = a2r * a1r - a2i * a1i
    ai = a2r * a1i + a2i * a1r
    br = a2r * b1r - a2i * b1i + b2r
    bi = a2r * b1i + a2i * b1r + b2i
    return (ar, ai, br, bi)

def s5_branch(u, a_re, a_im, log_dt, b_re, b_im, c_re, c_im, d_skip, w_glu, b_glu):
    f32 = jnp.float32
    uf = u.astype(f32)
    Bsz, L, _ = uf.shape
    ug = uf.reshape(Bsz, L, SSM_GROUPS, SSM_GROUP)
    lr, li = a_re.astype(f32), a_im.astype(f32)
    dt = jnp.exp(log_dt.astype(f32))[:, None]
    mag = jnp.exp(lr * dt)
    lbr, lbi = mag * jnp.cos(li * dt), mag * jnp.sin(li * dt)
    nr, ni = lbr - 1.0, lbi
    den = lr * lr + li * li
    qr = (nr * lr + ni * li) / den
    qi = (ni * lr - nr * li) / den
    br_, bi_ = b_re.astype(f32), b_im.astype(f32)
    bbr = qr[..., None] * br_ - qi[..., None] * bi_
    bbi = qr[..., None] * bi_ + qi[..., None] * br_
    bu_r = jnp.einsum('blgh,gph->blgp', ug, bbr)
    bu_i = jnp.einsum('blgh,gph->blgp', ug, bbi)
    ar = jnp.broadcast_to(lbr[None, None], bu_r.shape)
    ai = jnp.broadcast_to(lbi[None, None], bu_i.shape)
    _, _, s_r, s_i = lax.associative_scan(_scan_combine, (ar, ai, bu_r, bu_i), axis=1)
    y = (jnp.einsum('ghp,blgp->blgh', c_re.astype(f32), s_r)
         - jnp.einsum('ghp,blgp->blgh', c_im.astype(f32), s_i))
    y = y.reshape(Bsz, L, D_SSM) + d_skip.astype(f32)[None, None, :] * uf
    y = jax.nn.gelu(y)
    y = y * jax.nn.sigmoid(y @ w_glu.astype(f32) + b_glu.astype(f32))
    return y.astype(u.dtype)

def setup_inputs(seed: int = 0) -> dict:
    key = jax.random.key(seed)
    ks = jax.random.split(key, 20)
    f32 = jnp.float32
    x = jax.random.normal(ks[0], (BATCH, SEQ, D_MODEL), f32)
    norm_pre_g = 1.0 + 0.05 * jax.random.normal(ks[1], (D_MODEL,), f32)
    w_in = jax.random.normal(ks[2], (D_MODEL, N_IN), f32) * D_MODEL ** -0.5
    conv_w = jax.random.normal(ks[3], (CONV_WIDTH, D_CONV), f32) * CONV_WIDTH ** -0.5
    conv_b = 0.02 * jax.random.normal(ks[4], (D_CONV,), f32)
    n = jnp.arange(SSM_STATE, dtype=f32)[None, :]
    ssm_a_re = -0.5 + 0.01 * jax.random.normal(ks[5], (SSM_GROUPS, SSM_STATE), f32)
    ssm_a_im = math.pi * n + 0.01 * jax.random.normal(ks[6], (SSM_GROUPS, SSM_STATE), f32)
    ssm_log_dt = jax.random.uniform(ks[7], (SSM_GROUPS,), f32, math.log(DT_MIN), math.log(DT_MAX))
    bs = (2.0 * SSM_GROUP) ** -0.5
    ssm_b_re = jax.random.normal(ks[8], (SSM_GROUPS, SSM_STATE, SSM_GROUP), f32) * bs
    ssm_b_im = jax.random.normal(ks[9], (SSM_GROUPS, SSM_STATE, SSM_GROUP), f32) * bs
    cs = (2.0 * SSM_STATE) ** -0.5
    ssm_c_re = jax.random.normal(ks[10], (SSM_GROUPS, SSM_GROUP, SSM_STATE), f32) * cs
    ssm_c_im = jax.random.normal(ks[11], (SSM_GROUPS, SSM_GROUP, SSM_STATE), f32) * cs
    ssm_d = jax.random.normal(ks[12], (D_SSM,), f32)
    w_glu = jax.random.normal(ks[13], (D_SSM, D_SSM), f32) * D_SSM ** -0.5
    b_glu = 0.02 * jax.random.normal(ks[14], (D_SSM,), f32)
    w_out = jax.random.normal(ks[15], (D_MIX, D_MODEL), f32) * D_MIX ** -0.5
    norm_post_g = 1.0 + 0.05 * jax.random.normal(ks[16], (D_MODEL,), f32)
    return {"x": x, "norm_pre_g": norm_pre_g, "w_in": w_in, "conv_w": conv_w, "conv_b": conv_b,
            "ssm_a_re": ssm_a_re, "ssm_a_im": ssm_a_im, "ssm_log_dt": ssm_log_dt,
            "ssm_b_re": ssm_b_re, "ssm_b_im": ssm_b_im, "ssm_c_re": ssm_c_re, "ssm_c_im": ssm_c_im,
            "ssm_d": ssm_d, "w_glu": w_glu, "b_glu": b_glu, "w_out": w_out, "norm_post_g": norm_post_g}

def reference(x, norm_pre_g, w_in, conv_w, conv_b, ssm_a_re, ssm_a_im, ssm_log_dt,
              ssm_b_re, ssm_b_im, ssm_c_re, ssm_c_im, ssm_d, w_glu, b_glu, w_out, norm_post_g):
    for _ in range(DEPTH):
        h = rms_norm(x, norm_pre_g)
        proj = h @ w_in
        b_gate, c_gate, v, z_conv = jnp.split(proj[..., :4 * D_CONV], 4, axis=-1)
        u, z_ssm = jnp.split(proj[..., 4 * D_CONV:], 2, axis=-1)
        y_conv = b_gate * causal_dwconv(c_gate * v, conv_w, conv_b)
        y_conv = y_conv * jax.nn.silu(z_conv)
        y_ssm = s5_branch(u, ssm_a_re, ssm_a_im, ssm_log_dt, ssm_b_re, ssm_b_im,
                          ssm_c_re, ssm_c_im, ssm_d, w_glu, b_glu)
        y_ssm = y_ssm * jax.nn.silu(z_ssm)
        mix = jnp.concatenate([y_conv, y_ssm], axis=-1)
        x = x + rms_norm(mix @ w_out, norm_post_g)
    return x


_drawn_inputs = setup_inputs


def setup_inputs(seed=0):
    import zlib

    import numpy as np

    out = dict(_drawn_inputs(seed))
    spreads = {}
    factors = {'conv_b': 3.997,
     'ssm_a_re': 64.0,
     'ssm_a_im': 30.464,
     'ssm_log_dt': 30.84,
     'ssm_b_re': 42.744,
     'ssm_b_im': 42.784,
     'ssm_c_re': 42.432,
     'ssm_c_im': 43.448,
     'b_glu': 26.39}
    for name, (base, spread) in spreads.items():
        noise = np.random.default_rng([zlib.crc32(name.encode()), seed]).standard_normal(out[name].shape)
        drawn = base * np.exp(spread * noise) if base else spread * noise
        out[name] = __import__('jax').numpy.asarray(drawn.astype(out[name].dtype))
    for name, factor in factors.items():
        out[name] = (out[name] * factor).astype(out[name].dtype)
    return out
```

```python
import math

import concourse.bass as bass
from concourse import mybir

F32 = mybir.dt.float32
F32R = mybir.dt.float32r
I32 = mybir.dt.int32
ALU = mybir.AluOpType
ACT = mybir.ActivationFunctionType

P = 128
T = 512
D = 2048
DC = 1024
DS = 1024
G, S, H = 64, 64, 16
WIDTH = 3
EPS = 1e-6
KT = D // P
TT = T // P
J = DC // P
Q = 4
NQ = J * Q
KS = DS // P
KO = (DC + DS) // P
UK = 8
UC = UK * P

COL_B, COL_C, COL_V, COL_Z, COL_U, COL_G = 0, DC, 2 * DC, 3 * DC, 4 * DC, 4 * DC + DS

N_LOOP = 4
PER_J = 10
N_GATE = N_LOOP + PER_J * J
PER_P = 6
PAIRS = 3
N_GLU = N_GATE + PER_P * PAIRS
N_OUT = N_GLU + 2

C_IDENT, C_IOTA, C_MASK, C_HALF, C_HALFPI, C_QUARTER, C_COLS = 0, P, P + T, P + T + 2, P + T + 4, P + T + 5, P + T + 6
V_PRE, V_CW, V_CB, V_D, V_BG = 0, KT, KT + WIDTH * J, KT + (WIDTH + 1) * J, KT + (WIDTH + 2) * J
V_ROWS = V_BG + KS

TWO_PI = 6.2831850
INV_2PI = 1.0 / (2.0 * math.pi)
ROUND = 1.5 * 2.0 ** 23
ROUND15 = 1.5 * 2.0 ** 8
PI_A = 201.0 / 32.0
PI_B = 1014.0 / 2.0 ** 19
PI_C = 2.0 * math.pi - PI_A - PI_B
LN2_A = 355.0 / 512.0
LN2_B = math.log(2.0) - LN2_A


def build(nc, x, norm_pre_g, w_in, conv_w, conv_b, ssm_a_re, ssm_a_im, ssm_log_dt, ssm_b_re,
          ssm_b_im, ssm_c_re, ssm_c_im, ssm_d, w_glu, b_glu, w_out, norm_post_g, consts, out):
    at = [16512]

    def region(nbytes):
        start = at[0]
        at[0] += nbytes
        assert at[0] <= 229344, at[0]
        return start

    def place(name, shape, dtype, start, used=0):
        size = 4
        for n in shape[1:]:
            size *= n
        return nc.alloc_sbuf_tensor_at(name, shape, dtype, offset=start + used), used + (size + 31) // 32 * 32

    def own(name, shape, dtype=F32):
        size = 4
        for n in shape[1:]:
            size *= n
        return nc.alloc_sbuf_tensor_at(name, shape, dtype, offset=region((size + 31) // 32 * 32))

    w_raw = [own(f"w_raw{s}", [P, UC]) for s in range(2)]
    w_hi = [own(f"w_hi{s}", [P, UC], F32R) for s in range(2)]
    w_lo = [own(f"w_lo{s}", [P, UC], F32R) for s in range(2)]
    const = own("const", [P, C_COLS])
    cols = own("cols", [P, V_ROWS])
    mag = own("mag", [P, NQ])
    turn_hi = own("turn_hi", [P, NQ])
    turn_lo = own("turn_lo", [P, NQ])
    stats = own("stats", [P, 6, 8])
    v_sb = own("v_sb", [P, T])
    cv = own("cv", [P, T + WIDTH - 1])
    conv = own("conv", [P, T])
    sig = [own(f"sig{s}", [P, T]) for s in range(2)]
    b_split = own("b_split", [P, 3, 2 * P], F32R)
    c_cur = own("c_cur", [P, 2, 5 * P])

    r_h = region(2 * KT * T * 4)
    h_hi, n = place("h_hi", [P, KT, T], F32R, r_h)
    h_lo, n = place("h_lo", [P, KT, T], F32R, r_h, n)
    squares, _ = place("squares", [P, D], F32, r_h, KT * T * 4)
    x_res, n = place("x_res", [P, TT, D], F32, r_h)
    z_half, n = place("z_half", [P, TT, DC], F32, r_h, n)
    g_post, n = place("g_post", [P, D], F32, r_h, n)

    r_s = region(32 * 1024)
    x_sb, n = place("x_sb", [P, TT, D], F32, r_s)
    cos, n = place("cos", [P, Q, T], F32, r_s)
    sin, n = place("sin", [P, Q, T], F32, r_s, n)
    by_cos, n = place("by_cos", [P, 2, T], F32, r_s, n)
    by_sin, n = place("by_sin", [P, 2, T], F32, r_s, n)
    state = [None, None]
    state[0], n = place("state0", [P, 2, T], F32, r_s, n)
    state[1], n = place("state1", [P, 2, T], F32, r_s, n)
    assert n == 32 * 1024
    y_hi, n = place("y_hi", [P, KS, T], F32R, r_s)
    y_lo, n = place("y_lo", [P, KS, T], F32R, r_s, n)

    r_m = region(16 * 1024)
    b_all, n = place("b_all", [P, J, 2, P], F32, r_m)
    c_all, n = place("c_all", [P, 2, J, P], F32, r_m, n)
    glu = [None, None]
    glu[0], n = place("glu0", [P, T], F32, r_m)
    glu[1], n = place("glu1", [P, T], F32, r_m, n)
    m_hi, m_lo = [None, None], [None, None]
    for s in range(2):
        m_hi[s], n = place(f"m_hi{s}", [P, T], F32R, r_m, n)
        m_lo[s], n = place(f"m_lo{s}", [P, T], F32R, r_m, n)

    r_y = region(48 * 1024)
    y, n = place("y", [P, J, T], F32, r_y)
    mix, n = place("mix", [P, KO, T], F32, r_y, n)
    vec_rows, n = place("vec_rows", [V_ROWS, P], F32, r_y)
    par_rows, n = place("par_rows", [3 * NQ, P], F32, r_y, n)
    log_dt, n = place("log_dt", [P, 2], F32, r_y, n)
    par, n = place("par", [P, 24, NQ], F32, r_y, n)
    q_mask, n = place("q_mask", [P, 2, 2, NQ], F32, r_y, n)
    b_nat, n = place("b_nat", [P, 2, NQ, H], F32, r_y, n)
    b_pad, n = place("b_pad", [P, 2, NQ, 2, H], F32, r_y, n)
    b_tmp, n = place("b_tmp", [P, 2, NQ, H], F32, r_y, n)
    c_nat, n = place("c_nat", [P, 2, J, S], F32, r_y, n)
    c_pad, n = place("c_pad", [P, 2, J, 2, S], F32, r_y, n)
    assert n <= 48 * 1024, n
    u_stack, n = place("u_stack", [P, Q, T], F32R, r_y, (J + J) * T * 4)
    u_split, n = place("u_split", [P, 2, T], F32R, r_y, n)
    b_cur, n = place("b_cur", [P, Q, 2 * P], F32R, r_y, n)
    assert n == 48 * 1024
    exp2n, _ = place("exp2n", [P, NQ], I32, r_m)

    psum = nc.alloc_psum_tensor("psum", [P, 8, T], F32)
    bank_a, bank_b, bank_c, bank_y = 4, 5, 6, 7

    ident = const[:, C_IDENT:C_IDENT + P]
    iota = const[:, C_IOTA:C_IOTA + T]
    halfpi = const[:, C_HALFPI:C_HALFPI + 1]
    minus_quarter = const[:, C_QUARTER:C_QUARTER + 1]

    z_last, n = place("z_last", [P, 2, DC], F32, r_s)
    z_root, n = place("z_root", [P, 2, DC], F32, r_s, n)
    z_sum, n = place("z_sum", [P, TT, 4], F32, r_s, n)
    last_scratch, n = place("last_scratch", [P, T], F32, r_s, n)

    sem = nc.alloc_semaphore
    const_in, rows_in, ssm_in, res_in = sem("const_in"), sem("rows_in"), sem("ssm_in"), sem("res_in")
    gain_in = sem("gain_in")
    x_in = [sem(f"x_in{i}") for i in range(TT)]
    w_loaded = [sem(f"w_loaded{s}") for s in range(2)]
    w_hi_ready, w_lo_ready, units_done = sem("w_hi_ready"), sem("w_lo_ready"), sem("units_done")
    dve_step = sem("dve_step")
    rows_turned, dt_spread = sem("rows_turned"), sem("dt_spread")
    c_padded, c_turned, c_stored = sem("c_padded"), sem("c_turned"), sem("c_stored")
    b_padded = sem("b_padded")
    b_turned, b_stored = sem("b_turned"), sem("b_stored")
    turns_known, lam_trig = sem("turns_known"), sem("lam_trig")
    squared, mean_ready, root_ready, x_scaled = sem("squared"), sem("mean_ready"), sem("root_ready"), sem("x_scaled")
    x_turned, h_hi_ready, h_ready = sem("x_turned"), sem("h_hi_ready"), sem("h_ready")
    bu_ready, bu_free = sem("bu_ready"), sem("bu_free")
    rotated, scanned, unrotated = sem("rotated"), sem("scanned"), sem("unrotated")
    state_ready, state_free = sem("state_ready"), sem("state_free")
    turn_steps, phase_ready = sem("turn_steps"), sem("phase_ready")
    trig_steps, trig_ready = sem("trig_steps"), sem("trig_ready")
    c_cur_ready = sem("c_cur_ready")
    a_taken, b_taken, c_taken, y_taken = sem("a_taken"), sem("b_taken"), sem("c_taken"), sem("y_taken")
    tap_done = sem("tap_done")
    u_hi_ready, u_lo_ready, u_stacked = sem("u_hi_ready"), sem("u_lo_ready"), sem("u_stacked")
    b_hi_ready, b_split_ready, b_stacked = sem("b_hi_ready"), sem("b_split_ready"), sem("b_stacked")
    sig_ready, mix_ready = sem("sig_ready"), sem("mix_ready")
    gate_sig, gelu_done, y_hi_ready, y_lo_ready = sem("gate_sig"), sem("gelu_done"), sem("y_hi_ready"), sem("y_lo_ready")
    glu_sig, glu_mul, mix_gated = sem("glu_sig"), sem("glu_mul"), sem("mix_gated")
    m_hi_ready, m_lo_ready = sem("m_hi_ready"), sem("m_lo_ready")
    rows_done, z_even_copied, z_odd_copied = sem("rows_done"), sem("z_even_copied"), sem("z_odd_copied")
    z_squared, z_gained = sem("z_squared"), sem("z_gained")
    last_gained, last_squared = sem("last_gained"), sem("last_squared")
    out_mean, out_root, rstd_known, z_scaled = sem("out_mean"), sem("out_root"), sem("rstd_known"), sem("z_scaled")
    last_left_ready = sem("last_left_ready")
    left_ready, right_ready, out_stored = sem("left_ready"), sem("right_ready"), sem("out_stored")

    w_in_units = w_in.rearrange("(u k p) c -> u p k c", k=UK, p=P)
    w_glu_units = w_glu.rearrange("(k p) c -> p k c", p=P)
    w_out_units = w_out.rearrange("(k p) c -> k p c", p=P)

    def slot(n):
        return n % 2

    def rows_finished(engine, half, t):
        if t < TT - 1:
            engine.wait_ge(rows_done, (TT - 1) * half + t + 1)
        elif half == 0:
            engine.wait_ge(units_done, N_OUT + KO)
        else:
            engine.wait_ge(units_done, N_OUT + 2 * KO - 1)

    block_cm = nc.Block()
    block = block_cm.__enter__()

    @block.sync
    def _(sp):
        for i in range(TT):
            sp.dma_start(x_sb[:, i, :], x[0, i * P:(i + 1) * P, :]).then_inc(x_in[i], 16)

        def load(base, i, src):
            if not (isinstance(base, int) and base + i < 2):
                sp.wait_ge(w_lo_ready, base + i - 1)
            dst = w_raw[slot(i)][:, :]
            if len(src.shape) == 3:
                dst = dst.rearrange("p (k c) -> p k c", k=UK)
            sp.dma_start(dst, src).then_inc(w_loaded[slot(i)], 16)

        def tile_pair(base, i, col):
            for half in range(2):
                load(base, i + half, w_in_units[half, :, :, bass.ds(col, P)])

        def load_half(base, i, col):
            load(base, i, w_in_units[i % 2, :, :, bass.ds(col, P)])

        def stack(dst, src, again, stacked):
            for q in range(Q):
                rows = src[2 * H * q:2 * H * (q + 1), :, :].bitcast(F32)
                for half, part in enumerate((0, again)):
                    sp.dma_start(dst[half * P // 2:(half + 1) * P // 2, q, :].bitcast(F32),
                                 rows[:, part:part + 2, :]).then_inc(stacked, 16)

        def stack_b(j1):
            sp.wait_ge(b_split_ready, j1)
            stack(b_cur, b_split, 1, b_stacked)

        def stack_u(j1):
            sp.wait_ge(u_lo_ready, j1)
            stack(u_stack, u_split, 0, u_stacked)

        def channel_tile(j1, last):
            base = N_LOOP - PER_J + PER_J * j1
            load_half(base, 0, P * j1 + (COL_C - P))
            stack_u(j1)
            load_half(base, 1, P * j1 + (COL_C - P))
            tile_pair(base, 2, P * j1 + (COL_B - P))
            tile_pair(base, 4, P * j1 + (COL_Z - P))
            tile_pair(base, 6, COL_G if last else P * j1 + COL_U)
            load_half(base, 8, COL_G + P if last else P * j1 + COL_V)
            if not last:
                stack_b(j1 + 1)
            load_half(base, 9, COL_G + P if last else P * j1 + COL_V)

        tile_pair(0, 0, COL_U)
        tile_pair(0, 2, COL_V)
        stack_b(1)
        with sp.Fori(1, J) as j1:
            channel_tile(j1, False)
        channel_tile(J, True)
        with sp.Fori(1, PAIRS + 1) as p1:
            base = N_GATE - PER_P + PER_P * p1
            tile_pair(base, 0, 2 * P * p1 + COL_G)
            tile_pair(base, 2, 2 * P * p1 + COL_G + P)
            load(base, 4, w_glu_units[:, :, bass.ds(2 * P * p1 - 2 * P, P)])
            load(base, 5, w_glu_units[:, :, bass.ds(2 * P * p1 - P, P)])
        load(N_GLU, 0, w_glu_units[:, :, 6 * P:7 * P])
        load(N_GLU, 1, w_glu_units[:, :, 7 * P:8 * P])

        def out_unit(half, kp, i):
            load(N_OUT + KO * half + 2 * kp, i, w_out_units[bass.ds(2 * kp + i, 1), :, half * UC:(half + 1) * UC]
                 .rearrange("o p c -> (o p) c"))

        out_unit(0, 0, 0)
        sp.wait_ge(units_done, N_GLU - 2)
        sp.dma_start(g_post[:, :], norm_post_g.partition_broadcast(P)).then_inc(gain_in, 16)
        out_unit(0, 0, 1)
        x_cols = D // (KO // 2)
        x_tiles = x[0].rearrange("(t p) d -> p t d", p=P)
        with sp.Fori(1, KO // 2) as kp:
            for i in range(2):
                out_unit(0, kp, i)
            sp.dma_start(x_res[:, :, bass.ds(x_cols * kp, x_cols)],
                         x_tiles[:, :, bass.ds(x_cols * kp, x_cols)]).then_inc(res_in, 16)
        sp.dma_start(x_res[:, :, 0:x_cols], x_tiles[:, :, 0:x_cols]).then_inc(res_in, 16)
        with sp.Fori(0, KO // 2) as kp:
            for i in range(2):
                out_unit(1, kp, i)
        for t in range(TT):
            rows = out[0, t * P:(t + 1) * P, :]
            sp.wait_ge(right_ready, t + 1)
            sp.dma_start(rows[:, DC:], x_res[:, t, DC:]).then_inc(out_stored, 16)
            if t < TT - 1:
                sp.wait_ge(left_ready, t + 1)
            else:
                sp.wait_ge(last_left_ready, 1)
            sp.dma_start(rows[:, 0:DC], x_res[:, t, 0:DC]).then_inc(out_stored, 16)
        sp.wait_ge(out_stored, 2 * 16 * TT)

    @block.gpsimd
    def _(pool):
        pool.wait_ge(const_in, 16)
        pool.wait_ge(ssm_in, 64)
        for c in range(2):
            for a in range(2):
                step = pool.tensor_scalar(c_pad[:, c, :, a, :], c_nat[:, c, :, :],
                                          const[:, C_MASK + a:C_MASK + a + 1], 1.0, ALU.mult, ALU.mult)
        step.then_inc(c_padded, 1)

        def remainder(base, i):
            s = slot(i)
            pool.wait_ge(w_hi_ready, base + i + 1)
            pool.tensor_tensor(w_lo[s][:, :], w_raw[s][:, :], w_hi[s][:, :].bitcast(F32),
                               ALU.subtract).then_inc(w_lo_ready, 1)

        for i in range(N_LOOP):
            remainder(0, i)
        with pool.Fori(0, J) as j:
            for i in range(PER_J):
                remainder(N_LOOP + PER_J * j, i)
        with pool.Fori(0, PAIRS) as p:
            for i in range(PER_P):
                remainder(N_GATE + PER_P * p, i)
        with pool.Fori(0, KO // 2 + 2) as kp:
            for i in range(2):
                remainder(N_GLU + 2 * kp, i)
        for t in range(TT):
            for i in range(2):
                remainder(N_OUT + KO + 2 + 2 * t, i)
            if t == 0:
                pool.wait_ge(gain_in, 16)
            pool.wait_ge(z_squared, t + 1)
            pool.tensor_tensor(z_half[:, t, :], z_half[:, t, :], g_post[:, 0:DC], ALU.mult).then_inc(z_gained, 1)
        with pool.Fori(KO // 2 + 2 + TT, KO + 1) as kp:
            for i in range(2):
                remainder(N_GLU + 2 * kp, i)
        pool.wait_ge(res_in, 16 * (KO // 2))
        for t in range(TT - 1):
            pool.wait_ge(z_scaled, t + 1)
            pool.tensor_tensor(x_res[:, t, 0:DC], z_root[:, t % 2, :], x_res[:, t, 0:DC], ALU.add)\
                .then_inc(left_ready, 1)

    @block.scalar
    def _(act):
        act.dma_start(const[:, :], consts).then_inc(const_in, 16)
        rows = ((norm_pre_g.rearrange("(a p) -> a p", p=P), V_PRE, KT),
                (conv_w.rearrange("k (a p) -> (k a) p", p=P), V_CW, WIDTH * J),
                (conv_b.rearrange("(a p) -> a p", p=P), V_CB, J),
                (ssm_d.rearrange("(a p) -> a p", p=P), V_D, J),
                (b_glu.rearrange("(a p) -> a p", p=P), V_BG, KS))
        for src, row, count in rows:
            act.dma_start(vec_rows[row:row + count, :], src).then_inc(rows_in, 16)
        act.dma_start(par_rows[0:NQ, :], ssm_a_re.rearrange("(q a) p -> q (a p)", a=2)).then_inc(rows_in, 16)
        act.dma_start(par_rows[NQ:2 * NQ, :], ssm_a_im.rearrange("(q a) p -> q (a p)", a=2)).then_inc(rows_in, 16)
        act.dma_start(log_dt[2 * NQ:3 * NQ, :], ssm_log_dt.rearrange("(q a) -> q a", a=2)).then_inc(rows_in, 16)
        for c, src in enumerate((ssm_c_re, ssm_c_im)):
            act.dma_start(c_nat[:, c, :, :], src.rearrange("(j g) h p -> (g h) j p", g=2 * Q)).then_inc(ssm_in, 16)
        for c, src in enumerate((ssm_b_re, ssm_b_im)):
            act.dma_start(b_nat[:, c, :, :], src.rearrange("(q a) p h -> (a p) q h", a=2)).then_inc(ssm_in, 16)

        def rounded(base, i):
            s = slot(i)
            act.wait_ge(w_loaded[s], 8 * base + 16 * (i // 2 + 1))
            if not (isinstance(base, int) and base + i < 2):
                act.wait_ge(units_done, base + i - 1)
            act.activation(w_hi[s][:, :], w_raw[s][:, :], ACT.Copy).then_inc(w_hi_ready, 1)

        for i in range(TT):
            act.wait_ge(x_in[i], 16)
            act.activation(squares[:, :], x_sb[:, i, :], ACT.Square,
                           accum_out=stats[:, 0, i:i + 1]).then_inc(squared, 1)
            act.wait_ge(mean_ready, i + 1)
            act.activation(stats[:, 2, i:i + 1], stats[:, 1, i:i + 1], ACT.Sqrt).then_inc(root_ready, 1)
        for c in range(2):
            for half in range(2):
                act.wait_ge(c_turned, 2 * c + half + 1)
                act.activation(c_all[:, c, 4 * half:4 * half + 4, :],
                               psum[:, 2 * c + half, :].rearrange("p (j m) -> p j m", m=P),
                               ACT.Copy, scale=1.0 - 2.0 * c).then_inc(c_stored, 1)
        rounded(0, 0)
        rounded(0, 1)
        for k in range(KT):
            act.wait_ge(x_turned, k + 1)
            act.activation(h_hi[:, k, :], psum[:, k % 4, :], ACT.Copy,
                           scale=cols[:, V_PRE + k:V_PRE + k + 1]).then_inc(h_hi_ready, 1)
            if k == 11:
                act.wait_ge(turns_known, 1)
                act.activation(par[:, 12, :], par[:, 11, :], ACT.Sin, scale=TWO_PI).then_inc(lam_trig, 1)
                act.activation(par[:, 13, :], par[:, 11, :], ACT.Sin, scale=TWO_PI / 2).then_inc(lam_trig, 1)
        rounded(0, 2)

        def cosines(j, q):
            act.wait_ge(phase_ready, Q * j + q + 1)
            act.activation(sin[:, q, :], cos[:, q, :], ACT.Abs, bias=minus_quarter).then_inc(trig_steps, 1)
            act.wait_ge(trig_steps, 3 * (Q * j + q) + 1)
            act.activation(cos[:, q, :], cos[:, q, :], ACT.Abs).then_inc(trig_steps, 1)
            act.activation(sin[:, q, :], sin[:, q, :], ACT.Sin, scale=-TWO_PI, bias=halfpi).then_inc(trig_steps, 1)
            act.wait_ge(trig_steps, 3 * (Q * j + q) + 2)
            act.activation(cos[:, q, :], cos[:, q, :], ACT.Sin, scale=-TWO_PI, bias=halfpi).then_inc(trig_ready, 1)

        def round_u():
            act.activation(u_split[:, 0, :], psum[:, bank_a, :], ACT.Copy).then_inc(u_hi_ready, 1)

        def copy_v():
            act.activation(v_sb[:, :], psum[:, bank_b, :], ACT.Copy).then_inc(b_taken, 1)

        act.wait_ge(units_done, 2)
        round_u()
        rounded(0, 3)
        for bank in range(4):
            act.wait_ge(b_turned, bank + 1)
            act.activation(b_all[:, 2 * bank:2 * bank + 2, :, :],
                           psum[:, bank, :].rearrange("p (j c m) -> p j c m", j=2, c=2),
                           ACT.Copy).then_inc(b_stored, 1)
        rounded(N_LOOP, 0)
        for q in range(Q):
            cosines(0, q)
        act.wait_ge(units_done, N_LOOP)
        copy_v()
        rounded(N_LOOP, 1)

        def z_sigmoid(j):
            act.wait_ge(mix_ready, j + 1)
            act.activation(sig[0][:, :], psum[:, bank_b, :], ACT.Sigmoid).then_inc(sig_ready, 1)

        with act.Fori(0, J - 1) as j:
            base = N_LOOP + PER_J * j
            for i in range(PER_J):
                rounded(base, i + 2)
                if i == 3:
                    cosines(j + 1, 0)
                elif i == 5:
                    z_sigmoid(j)
                elif i == 6:
                    cosines(j + 1, 1)
                elif i == 7:
                    act.wait_ge(bu_ready, Q * (j + 1))
                    round_u()
                elif i == 8:
                    cosines(j + 1, 2)
                elif i == 9:
                    act.wait_ge(c_taken, j + 2)
                    copy_v()
                    cosines(j + 1, 3)
        j, base = J - 1, N_LOOP + PER_J * (J - 1)
        for i in range(PER_J):
            rounded(base, i + 2)
            if i == 5:
                z_sigmoid(j)
            elif i == 7:
                act.activation(sig[1][:, :], psum[:, bank_a, :], ACT.Sigmoid).then_inc(gate_sig, 1)
            elif i == 9:
                act.wait_ge(mix_ready, j + 2)
                act.activation(sig[0][:, :], psum[:, bank_b, :], ACT.Sigmoid).then_inc(gate_sig, 1)
        for half in range(2):
            act.wait_ge(y_taken, J + 1)
            part = y[:, 4 * half:4 * half + 4, :]
            act.activation(part, part, ACT.Gelu_apprx_tanh).then_inc(gelu_done, 1)
        with act.Fori(0, PAIRS) as p:
            base = N_GATE + PER_P * p
            for i in range(PER_P):
                rounded(base, i + 2)
                if i == 1:
                    act.wait_ge(a_taken, 2 * J + 1 + p)
                    act.activation(sig[1][:, :], psum[:, bank_a, :], ACT.Sigmoid).then_inc(gate_sig, 1)
                elif i == 3:
                    act.wait_ge(b_taken, 2 * J + 1 + p)
                    act.activation(sig[0][:, :], psum[:, bank_b, :], ACT.Sigmoid).then_inc(gate_sig, 1)
                elif i == 4:
                    act.wait_ge(c_taken, J + 2 + p)
                    act.activation(glu[0][:, :], glu[0][:, :], ACT.Sigmoid).then_inc(glu_sig, 1)
                elif i == 5:
                    act.wait_ge(y_taken, J + 2 + p)
                    act.activation(glu[1][:, :], glu[1][:, :], ACT.Sigmoid).then_inc(glu_sig, 1)
        for i, bank_sem in enumerate((c_taken, y_taken)):
            rounded(N_GLU, i + 2)
            act.wait_ge(bank_sem, J + 2 + PAIRS)
            act.activation(glu[i][:, :], glu[i][:, :], ACT.Sigmoid).then_inc(glu_sig, 1)
        with act.Fori(0, KO // 2 - 1) as kp:
            for i in range(2):
                rounded(N_OUT + 2 * kp, i + 2)
        rounded(N_OUT + KO - 2, 2)
        for t in range(TT):
            rows_finished(act, 0, t)
            act.activation(z_half[:, t, T:], psum[:, 2 * t + 1, :], ACT.Copy).then_inc(z_odd_copied, 1)
        rounded(N_OUT + KO - 2, 3)
        for t in range(TT):
            act.wait_ge(z_odd_copied, t + 1)
            act.wait_ge(z_even_copied, t + 1)
            if t >= 2:
                act.wait_ge(z_squared, t - 1)
            act.activation(z_root[:, t % 2, :], z_half[:, t, :], ACT.Square,
                           accum_out=z_sum[:, t, 0:1]).then_inc(z_squared, 1)
        with act.Fori(0, KO // 2 - 1) as kp:
            for i in range(2):
                rounded(N_OUT + KO + 2 * kp, i + 2)
        act.wait_ge(z_gained, TT)
        for t in range(TT):
            rows_finished(act, 1, t)
            for b in range(2):
                if b:
                    act.wait_ge(last_gained, 2 * t + 1)
                if t or b:
                    act.wait_ge(last_squared, 2 * t + b)
                act.activation(last_scratch[:, :], psum[:, 2 * t + 1 - b, :], ACT.Square,
                               accum_out=z_sum[:, t, 1 + b:2 + b]).then_inc(last_squared, 1)
            act.wait_ge(out_mean, t + 1)
            act.activation(stats[:, 4, t:t + 1], stats[:, 3, t:t + 1], ACT.Sqrt).then_inc(out_root, 1)
            if t < TT - 1:
                act.wait_ge(rstd_known, t + 1)
                if t >= 2:
                    act.wait_ge(left_ready, t - 1)
                else:
                    act.wait_ge(z_squared, TT)
                act.activation(z_root[:, t % 2, :], z_half[:, t, :], ACT.Copy,
                               scale=stats[:, 1, t:t + 1]).then_inc(z_scaled, 1)

    @block.vector
    def _(dve):
        steps = [0]

        def link(ins):
            steps[0] += 1
            ins.then_inc(dve_step, 1)
            dve.wait_ge(dve_step, steps[0])

        def ts(out_, in_, s1, op0, s2=None, op1=None):
            if op1 is None:
                return dve.tensor_scalar(out_, in_, s1, None, op0)
            return dve.tensor_scalar(out_, in_, s1, s2, op0, op1)

        def stt(out_, in0, scalar, op0, in1, op1):
            return dve.scalar_tensor_tensor(out=out_, in0=in0, scalar=scalar, in1=in1, op0=op0, op1=op1)

        tt = dve.tensor_tensor
        mult, add, sub = ALU.mult, ALU.add, ALU.subtract

        dve.memset(cv[:, 0:WIDTH - 1], 0.0).then_inc(mix_ready, 1)
        link(dve.memset(c_cur[:, :, :], 0.0))
        dve.wait_ge(rows_in, 8 * 16)
        dve.tensor_copy(par_rows[2 * NQ:3 * NQ, :].rearrange("q (a p) -> q a p", a=2),
                        log_dt[2 * NQ:3 * NQ, :].unsqueeze(2).to_broadcast([NQ, 2, S])).then_inc(dt_spread, 1)
        dve.wait_ge(rows_turned, 1)
        dve.tensor_copy(cols[:, :], psum[:, bank_c, 0:V_ROWS]).then_inc(c_taken, 1)
        dve.wait_ge(rows_turned, 2)
        dve.tensor_copy(par[:, 0:3, :], psum[:, bank_y, 0:3 * NQ].rearrange("p (a q) -> p a q", a=3)).then_inc(y_taken, 1)
        dve.wait_ge(c_taken, 1)
        dve.wait_ge(y_taken, 1)
        v = [par[:, i, :] for i in range(24)]
        (a_re, a_im, ldt, dt, arg, n, r, acc, two_n, expm1, th, turns, sin_th, sin_half, cosm1, cos_th,
         nr, ni, den, qr, qi, t0, t1, t2) = v

        def exponential(x_, out_, minus_one=None):
            link(ts(arg, x_, -88.0, ALU.max, 89.0, ALU.min))
            link(ts(n, arg, 1.0 / math.log(2.0), mult, ROUND, add))
            link(ts(n, n, -ROUND, add, 127.0, ALU.min))
            link(stt(r, n, -LN2_A, mult, arg, add))
            link(stt(r, n, -LN2_B, mult, r, add))
            link(ts(acc, r, 1.0 / math.factorial(9), mult))
            for k in range(8, 0, -1):
                link(stt(acc, acc, 1.0 / math.factorial(k), add, r, mult))
            link(ts(exp2n[:, :], n, 127.0, add, 2.0 ** 23, mult))
            two = exp2n[:, :].bitcast(F32)
            link(stt(out_, acc, 1.0, add, two, mult))
            if minus_one is not None:
                link(ts(two_n, two, -1.0, add))
                link(tt(t0, acc, two, mult))
                link(tt(minus_one, t0, two_n, add))

        exponential(ldt, dt)
        link(tt(th, a_im, dt, mult))
        link(ts(n, th, INV_2PI, mult, ROUND, add))
        link(ts(n, n, -ROUND, add))
        link(stt(r, n, -PI_A, mult, th, add))
        link(stt(r, n, -PI_B, mult, r, add))
        link(stt(r, n, -PI_C, mult, r, add))
        link(ts(turns, r, INV_2PI, mult))
        link(ts(turns, turns, 0.5, ALU.min, -0.5, ALU.max))
        dve.tensor_scalar(turn_hi[:, :], turns, ROUND15, -ROUND15, add, add).then_inc(turns_known, 1)
        dve.wait_ge(turns_known, 1)
        link(tt(turn_lo[:, :], turns, turn_hi[:, :], sub))
        link(tt(t1, a_re, dt, mult))
        exponential(t1, mag[:, :], expm1)

        def inverse_root(mean, root, inverse, known=None):
            link(dve.reciprocal(inverse, root))
            link(ts(stats[:, 5, 0:1], inverse, inverse, mult, mean, mult))
            link(ts(stats[:, 5, 1:2], stats[:, 5, 0:1], -0.5, mult, 1.5, add))
            step = tt(inverse, inverse, stats[:, 5, 1:2], mult)
            if known is None:
                link(step)
            else:
                step.then_inc(known, 1)

        for i in range(TT):
            dve.wait_ge(squared, i + 1)
            ts(stats[:, 1, i:i + 1], stats[:, 0, i:i + 1], 1.0 / D, mult, EPS, add).then_inc(mean_ready, 1)
            dve.wait_ge(root_ready, i + 1)
            inverse_root(stats[:, 1, i:i + 1], stats[:, 2, i:i + 1], stats[:, 3, i:i + 1])
            ts(x_sb[:, i, :], x_sb[:, i, :], stats[:, 3, i:i + 1], mult).then_inc(x_scaled, 1)

        for k in range(KT):
            dve.wait_ge(h_hi_ready, k + 1)
            stt(h_lo[:, k, :], psum[:, k % 4, :], cols[:, V_PRE + k:V_PRE + k + 1], mult,
                h_hi[:, k, :].bitcast(F32), sub).then_inc(h_ready, 1)

        dve.wait_ge(lam_trig, 2)
        link(stt(cosm1, sin_half, -2.0, mult, sin_half, mult))
        link(ts(cos_th, cosm1, 1.0, add))
        link(tt(t0, expm1, cos_th, mult))
        link(tt(nr, t0, cosm1, add))
        link(tt(ni, mag[:, :], sin_th, mult))
        link(tt(t0, a_re, a_re, mult))
        link(tt(t1, a_im, a_im, mult))
        link(tt(den, t0, t1, add))
        link(dve.reciprocal(den, den))
        link(tt(t0, nr, a_re, mult))
        link(tt(t1, ni, a_im, mult))
        link(tt(qr, t0, t1, add))
        link(tt(qr, qr, den, mult))
        link(tt(t0, ni, a_re, mult))
        link(tt(t1, nr, a_im, mult))
        link(tt(qi, t0, t1, sub))
        link(tt(qi, qi, den, mult))
        for a in range(2):
            ts(q_mask[:, 0, a, :], qr, const[:, C_HALF + a:C_HALF + a + 1], mult)
            link(ts(q_mask[:, 1, a, :], qi, const[:, C_HALF + a:C_HALF + a + 1], mult))

        def over_h(c, a):
            return q_mask[:, c, a, :].unsqueeze(2).to_broadcast([P, NQ, H])

        dve.wait_ge(ssm_in, 64)
        for a in range(2):
            for c in range(2):
                tt(b_tmp[:, 0, :, :], b_nat[:, c, :, :], over_h(0, a), mult)
                link(tt(b_tmp[:, 1, :, :], b_nat[:, 1 - c, :, :], over_h(1, a), mult))
                step = tt(b_pad[:, c, :, a, :], b_tmp[:, 0, :, :], b_tmp[:, 1, :, :], add if c else sub)
                step.then_inc(b_padded, 1)
                dve.wait_ge(b_padded, 2 * a + c + 1)

        def phases(j, q):
            at_ = Q * j + q
            hi = turn_hi[:, bass.ds(at_, 1)]
            lo = turn_lo[:, bass.ds(at_, 1)]
            ts(sin[:, q, :], iota, hi, mult, -0.125, add).then_inc(turn_steps, 1)
            dve.wait_ge(turn_steps, 3 * at_ + 1)
            ts(sin[:, q, :], sin[:, q, :], ROUND, add, -ROUND, add).then_inc(turn_steps, 1)
            dve.wait_ge(turn_steps, 3 * at_ + 2)
            stt(cos[:, q, :], iota, hi, mult, sin[:, q, :], sub).then_inc(turn_steps, 1)
            dve.wait_ge(turn_steps, 3 * at_ + 3)
            stt(cos[:, q, :], iota, lo, mult, cos[:, q, :], add).then_inc(phase_ready, 1)

        def input_matrix(j):
            src = b_all[:, bass.ds(j, 1), :, :].rearrange("p o c m -> p (o c m)")
            ts(b_split[:, 2, :], src, 1.0, mult).then_inc(b_hi_ready, 1)
            ts(b_split[:, 0, :], src, 1.0, mult).then_inc(b_hi_ready, 1)
            dve.wait_ge(b_hi_ready, 2 * j + 2)
            tt(b_split[:, 1, :], src, b_split[:, 0, :].bitcast(F32), sub).then_inc(b_split_ready, 1)

        def output_matrix(j):
            dst = c_cur[:, :, :].rearrange("p c (q r) -> p c q r", r=P + 2 * H)[:, :, :, 0:2 * H]
            src = c_all[:, :, bass.ds(j, 1), :].rearrange("p c o (q r) -> p (c o) q r", r=2 * H)
            ts(dst, src, 1.0, mult).then_inc(c_cur_ready, 1)

        def skip(j):
            dve.wait_ge(u_hi_ready, j + 1)
            tt(u_split[:, 1, :], psum[:, bank_a, :], u_split[:, 0, :].bitcast(F32), sub).then_inc(u_lo_ready, 1)
            ts(y[:, bass.ds(j, 1), :].rearrange("p o t -> p (o t)"), psum[:, bank_a, :],
               cols[:, bass.ds(V_D + j, 1)], mult).then_inc(a_taken, 1)

        def over_parts(tab, q):
            return tab[:, q, :].unsqueeze(1).to_broadcast([P, 2, T])

        def scan(j, q):
            at_ = Q * j + q
            bu = psum[:, 2 * (q % 2):2 * (q % 2) + 2, :]
            st = state[q % 2]
            dve.wait_ge(bu_ready, at_ + 1)
            dve.wait_ge(trig_ready, at_ + 1)
            if q:
                dve.wait_ge(state_ready, at_)
            else:
                dve.wait_ge(c_cur_ready, j + 1)
            tt(by_cos[:, :, :], bu, over_parts(cos, q), mult)
            tt(by_sin[:, :, :], bu, over_parts(sin, q), mult).then_inc(bu_free, 1)
            dve.wait_ge(bu_free, at_ + 3)
            dve.wait_ge(state_free, at_ + 1)
            tt(st[:, 0, :], by_cos[:, 0, :], by_sin[:, 1, :], add).then_inc(rotated, 1)
            tt(st[:, 1, :], by_cos[:, 1, :], by_sin[:, 0, :], sub).then_inc(rotated, 1)
            size = mag[:, bass.ds(at_, 1)].to_broadcast([P, T])
            for c in range(2):
                dve.wait_ge(rotated, 2 * at_ + 1 + c)
                dve.tensor_tensor_scan(st[:, c, :], size, st[:, c, :], 0.0, mult, add).then_inc(scanned, 1)
            dve.wait_ge(scanned, 2 * at_ + 2)
            tt(by_cos[:, :, :], st[:, :, :], over_parts(cos, q), mult)
            tt(by_sin[:, :, :], st[:, :, :], over_parts(sin, q), mult).then_inc(unrotated, 1)
            dve.wait_ge(unrotated, at_ + 1)
            tt(st[:, 0, :], by_cos[:, 0, :], by_sin[:, 1, :], sub)
            tt(st[:, 1, :], by_cos[:, 1, :], by_sin[:, 0, :], add).then_inc(state_ready, 1)

        skip(0)
        dve.wait_ge(x_turned, KT)
        for q in range(Q):
            phases(0, q)
        dve.wait_ge(c_stored, 4)
        output_matrix(0)
        dve.wait_ge(b_stored, 4)
        input_matrix(0)
        dve.wait_ge(b_split_ready, 1)
        dve.memset(stats[:, 5, 2:3], 0.0).then_inc(bu_free, 2)

        def conv_taps(j):
            base = N_LOOP + PER_J * j
            dve.wait_ge(units_done, base + 2)
            dve.wait_ge(b_taken, 2 * j + 1)
            tt(cv[:, WIDTH - 1:], psum[:, bank_c, :], v_sb[:, :], mult).then_inc(c_taken, 1)
            dve.wait_ge(c_taken, j + 2)
            w = [cols[:, bass.ds(V_CW + J * k + j, 1)] for k in range(WIDTH)]
            ts(conv[:, :], cv[:, 0:T], w[0], mult, cols[:, bass.ds(V_CB + j, 1)], add).then_inc(tap_done, 1)
            for k in range(1, WIDTH):
                dve.wait_ge(tap_done, WIDTH * j + k)
                stt(conv[:, :], cv[:, k:k + T], w[k], mult, conv[:, :], add).then_inc(tap_done, 1)

        def gate_b(j):
            dve.wait_ge(units_done, N_LOOP + PER_J * j + 4)
            dve.wait_ge(tap_done, WIDTH * (j + 1))
            tt(conv[:, :], psum[:, bank_a, :], conv[:, :], mult).then_inc(a_taken, 1)

        def gate_z(j):
            dve.wait_ge(sig_ready, j + 1)
            dve.wait_ge(a_taken, 2 * j + 2)
            tt(conv[:, :], psum[:, bank_b, :], conv[:, :], mult).then_inc(b_taken, 1)
            dve.wait_ge(b_taken, 2 * j + 2)
            tt(mix[:, bass.ds(j, 1), :].rearrange("p o t -> p (o t)"), conv[:, :], sig[0][:, :], mult)\
                .then_inc(mix_ready, 1)

        def finish_y(j):
            dve.wait_ge(state_free, Q * (j + 1) + 2)
            dst = y[:, bass.ds(j, 1), :].rearrange("p o t -> p (o t)")
            tt(dst, psum[:, bank_y, :], dst, add).then_inc(y_taken, 1)

        def gate(m, bank, s, taken):
            dve.wait_ge(gate_sig, m + 1)
            tt(mix[:, bass.ds(J + m, 1), :].rearrange("p o t -> p (o t)"), psum[:, bank, :], sig[s][:, :], mult)\
                .then_inc(taken, 1)

        with dve.Fori(0, J - 1) as j:
            scan(j, 0)
            conv_taps(j)
            phases(j + 1, 0)
            scan(j, 1)
            gate_b(j)
            phases(j + 1, 1)
            scan(j, 2)
            gate_z(j)
            dve.wait_ge(bu_ready, Q * (j + 1))
            input_matrix(j + 1)
            scan(j, 3)
            phases(j + 1, 2)
            phases(j + 1, 3)
            skip(j + 1)
            finish_y(j)
            output_matrix(j + 1)
        j = J - 1
        scan(j, 0)
        conv_taps(j)
        scan(j, 1)
        gate_b(j)
        scan(j, 2)
        gate_z(j)
        scan(j, 3)
        gate(0, bank_a, 1, a_taken)
        gate(1, bank_b, 0, b_taken)
        finish_y(j)
        dve.wait_ge(gelu_done, 2)
        ts(y_hi[:, :, :], y[:, :, :], 1.0, mult).then_inc(y_hi_ready, 1)
        dve.wait_ge(y_hi_ready, 1)
        tt(y_lo[:, :, :], y[:, :, :], y_hi[:, :, :].bitcast(F32), sub).then_inc(y_lo_ready, 1)

        def split_mix(half, kp, i):
            at_ = KO * half + 2 * kp + i
            if isinstance(kp, int) and KO * half + kp == 0:
                dve.wait_ge(mix_ready, 1 + at_ + 1)
            else:
                dve.wait_ge(units_done, N_OUT - 1 + at_)
            src = mix[:, bass.ds(2 * kp + i, 1), :].rearrange("p o t -> p (o t)")
            ts(m_hi[i][:, :], src, 1.0, mult).then_inc(m_hi_ready, 1)
            dve.wait_ge(m_hi_ready, at_ + 1)
            tt(m_lo[i][:, :], src, m_hi[i][:, :].bitcast(F32), sub).then_inc(m_lo_ready, 1)

        for i in range(2):
            split_mix(0, 0, i)

        def glu_bias(base, m, i, bank, taken):
            dve.wait_ge(units_done, base + 5 + i)
            ts(glu[i][:, :], psum[:, bank, :], cols[:, bass.ds(V_BG + m, 1)], add).then_inc(taken, 1)

        def glu_apply(m, i):
            dve.wait_ge(glu_sig, m + 1)
            tt(glu[i][:, :], y[:, bass.ds(m, 1), :].rearrange("p o t -> p (o t)"), glu[i][:, :], mult)\
                .then_inc(glu_mul, 1)
            dve.wait_ge(glu_mul, m + 1)
            dst = mix[:, bass.ds(J + m, 1), :].rearrange("p o t -> p (o t)")
            tt(dst, dst, glu[i][:, :], mult).then_inc(mix_gated, 1)

        with dve.Fori(0, PAIRS) as p:
            base = N_GATE + PER_P * p
            gate(2 * p + 2, bank_a, 1, a_taken)
            gate(2 * p + 3, bank_b, 0, b_taken)
            glu_bias(base, 2 * p, 0, bank_c, c_taken)
            glu_apply(2 * p, 0)
            glu_bias(base, 2 * p + 1, 1, bank_y, y_taken)
            glu_apply(2 * p + 1, 1)
        glu_bias(N_GLU - 4, 6, 0, bank_c, c_taken)
        glu_apply(6, 0)
        glu_bias(N_GLU - 4, 7, 1, bank_y, y_taken)
        glu_apply(7, 1)

        dve.wait_ge(mix_gated, J)
        with dve.Fori(1, KO // 2) as kp:
            for i in range(2):
                split_mix(0, kp, i)
        split_mix(1, 0, 0)
        for t in range(TT):
            rows_finished(dve, 0, t)
            ts(z_half[:, t, 0:T], psum[:, 2 * t, :], 1.0, mult).then_inc(z_even_copied, 1)
        split_mix(1, 0, 1)
        with dve.Fori(1, KO // 2) as kp:
            for i in range(2):
                split_mix(1, kp, i)
        dve.wait_ge(z_squared, TT)
        for t in range(TT):
            link(ts(stats[:, 2, t:t + 1], z_sum[:, t, 0:1], 1.0 / D, mult, EPS, add))
        dve.wait_ge(gain_in, 16)
        dve.wait_ge(res_in, 16 * (KO // 2))
        for t in range(TT):
            zl = z_last[:, t % 2, :]
            rows_finished(dve, 1, t)
            if t >= 2:
                dve.wait_ge(right_ready, t - 1)
            for b in range(2):
                if b:
                    dve.wait_ge(last_squared, 2 * t + 1)
                tt(zl[:, b * T:(b + 1) * T], psum[:, 2 * t + b, :], g_post[:, DC + b * T:DC + (b + 1) * T],
                   mult).then_inc(last_gained, 1)
            dve.wait_ge(last_squared, 2 * t + 2)
            link(tt(stats[:, 3, t:t + 1], z_sum[:, t, 1:2], z_sum[:, t, 2:3], add))
            stt(stats[:, 3, t:t + 1], stats[:, 3, t:t + 1], 1.0 / D, mult, stats[:, 2, t:t + 1], add)\
                .then_inc(out_mean, 1)
            dve.wait_ge(out_root, t + 1)
            inverse_root(stats[:, 3, t:t + 1], stats[:, 4, t:t + 1], stats[:, 1, t:t + 1], rstd_known)
            dve.wait_ge(rstd_known, t + 1)
            dve.wait_ge(last_gained, 2 * t + 2)
            rstd = stats[:, 1, t:t + 1]
            stt(x_res[:, t, DC:], zl, rstd, mult, x_res[:, t, DC:], add).then_inc(right_ready, 1)
            if t == TT - 1:
                dve.wait_ge(z_gained, TT)
                stt(x_res[:, t, 0:DC], z_half[:, t, :], rstd, mult, x_res[:, t, 0:DC], add).then_inc(last_left_ready, 1)

    @block.tensor
    def _(pe):
        def turn(dst, src, k):
            return pe.transpose(dst, src, ident[0:k, 0:k])

        pe.wait_ge(const_in, 16)
        pe.wait_ge(rows_in, 8 * 16)
        turn(psum[:, bank_c, 0:V_ROWS], vec_rows[:, :], V_ROWS).then_inc(rows_turned, 1)
        pe.wait_ge(dt_spread, 1)
        turn(psum[:, bank_y, 0:3 * NQ], par_rows[:, :], 3 * NQ).then_inc(rows_turned, 1)
        pe.wait_ge(c_padded, 1)
        for c in range(2):
            for j in range(J):
                ins = turn(psum[:, 2 * c + j // 4, (j % 4) * P:(j % 4 + 1) * P], c_pad[:, c, j, :, :], P)
                if j % 4 == 3:
                    ins.then_inc(c_turned, 1)

        def product(bank, k, kt, s, first, last, a_hi=h_hi, a_lo=h_lo):
            wh = w_hi[s][:, k * P:(k + 1) * P]
            wl = w_lo[s][:, k * P:(k + 1) * P]
            pe.matmul(psum[:, bank, :], wh, a_hi[:, kt, :], start=first, stop=False)
            pe.matmul(psum[:, bank, :], wh, a_lo[:, kt, :], start=False, stop=False)
            return pe.matmul(psum[:, bank, :], wl, a_hi[:, kt, :], start=False, stop=last)

        def unit(base, i, bank, half, first):
            pe.wait_ge(w_lo_ready, base + i + 1)
            for k in range(UK):
                ins = product(bank, k, UK * half + k, slot(i), first and k == 0, not first and k == UK - 1)
            ins.then_inc(units_done, 1)

        def tile(base, i, bank):
            unit(base, i, bank, 0, True)
            unit(base, i + 1, bank, 1, False)

        pe.wait_ge(x_scaled, TT)
        for k in range(KT + 2):
            if k < KT:
                if k < 4:
                    pe.wait_ge(c_stored, k + 1)
                else:
                    pe.wait_ge(h_ready, k - 3)
                for t in range(TT):
                    ins = turn(psum[:, k % 4, t * P:(t + 1) * P], x_sb[:, t, k * P:(k + 1) * P], P)
                ins.then_inc(x_turned, 1)
            if k >= 2:
                kt = k - 2
                if kt % UK == 0:
                    pe.wait_ge(w_lo_ready, kt // UK + 1)
                pe.wait_ge(h_ready, kt + 1)
                ins = product(bank_a, kt % UK, kt, kt // UK, kt == 0, kt == KT - 1)
                if kt % UK == UK - 1:
                    ins.then_inc(units_done, 1)
        unit(0, 2, bank_b, 0, True)
        pe.wait_ge(b_padded, 4)
        for j in range(J):
            for c in range(2):
                dst = psum[:, j // 2, ((j % 2) * 2 + c) * P:((j % 2) * 2 + c + 1) * P]
                ins = turn(dst, b_pad[:, c, Q * j:Q * j + Q, :, :], P)
                if j == 0 and c == 0:
                    ins.then_inc(state_free, 2)
                elif j % 2 and c:
                    ins.then_inc(b_turned, 1)
        unit(0, 3, bank_b, 1, False)

        def inputs(j, q):
            at_ = Q * j + q
            if q == 0:
                pe.wait_ge(b_stacked, 16 * 2 * Q * (j + 1))
                pe.wait_ge(u_stacked, 16 * 2 * Q * (j + 1))
            pe.wait_ge(bu_free, at_ + 1)
            for c in range(2):
                ins = pe.matmul(psum[:, 2 * (q % 2) + c, :], b_cur[:, q, c * P:(c + 1) * P], u_stack[:, q, :],
                                start=True, stop=True)
            ins.then_inc(bu_ready, 1)

        def outputs(j, q):
            if q == 0:
                pe.wait_ge(c_cur_ready, j + 1)
                pe.wait_ge(y_taken, j + 1)
            pe.wait_ge(state_ready, Q * j + q + 1)
            for c in range(2):
                ins = pe.matmul(psum[:, bank_y, :], c_cur[:, c, q * P:(q + 1) * P], state[q % 2][:, c, :],
                                start=(q == 0 and c == 0), stop=(q == Q - 1 and c == 1))
            ins.then_inc(state_free, 1)

        def channel_tile(j):
            base = N_LOOP + PER_J * j
            pe.wait_ge(c_taken, j + 1)
            unit(base, 0, bank_c, 0, True)
            inputs(j, 0)
            unit(base, 1, bank_c, 1, False)
            inputs(j, 1)
            pe.wait_ge(a_taken, 2 * j + 1)
            tile(base, 2, bank_a)
            inputs(j, 2)
            outputs(j, 0)
            pe.wait_ge(b_taken, 2 * j + 1)
            tile(base, 4, bank_b)
            inputs(j, 3)
            outputs(j, 1)
            pe.wait_ge(a_taken, 2 * j + 2)
            tile(base, 6, bank_a)
            outputs(j, 2)
            pe.wait_ge(b_taken, 2 * j + 2)
            tile(base, 8, bank_b)
            outputs(j, 3)

        with pe.Fori(0, J) as j:
            channel_tile(j)

        def glu_tile(base, i, bank):
            pe.wait_ge(w_lo_ready, base + i + 1)
            for k in range(KS):
                ins = product(bank, k, k, slot(i), k == 0, k == KS - 1, y_hi, y_lo)
            ins.then_inc(units_done, 1)

        with pe.Fori(0, PAIRS) as p:
            base = N_GATE + PER_P * p
            pe.wait_ge(a_taken, 2 * J + 1 + p)
            tile(base, 0, bank_a)
            pe.wait_ge(b_taken, 2 * J + 1 + p)
            tile(base, 2, bank_b)
            pe.wait_ge(y_lo_ready, 1)
            pe.wait_ge(c_taken, J + 1 + p)
            glu_tile(base, 4, bank_c)
            pe.wait_ge(y_taken, J + 1 + p)
            glu_tile(base, 5, bank_y)
        pe.wait_ge(c_taken, J + 1 + PAIRS)
        glu_tile(N_GLU, 0, bank_c)
        pe.wait_ge(y_taken, J + 1 + PAIRS)
        glu_tile(N_GLU, 1, bank_y)

        def out_unit(half, kp, i, first):
            at_ = KO * half + 2 * kp + i
            pe.wait_ge(w_lo_ready, N_OUT + at_ + 1)
            pe.wait_ge(m_lo_ready, at_ + 1)
            start = bool(first) and i == 0
            for t in range(TT):
                mh, ml = m_hi[i][:, t * P:(t + 1) * P], m_lo[i][:, t * P:(t + 1) * P]
                for b in range(2):
                    bank = psum[:, 2 * t + b, :]
                    wh, wl = w_hi[i][:, b * T:(b + 1) * T], w_lo[i][:, b * T:(b + 1) * T]
                    if start and half == 0 and t >= 2 and b == 0:
                        if t == 2:
                            pe.wait_ge(a_taken, 2 * J + 1 + PAIRS)
                            pe.wait_ge(b_taken, 2 * J + 1 + PAIRS)
                        else:
                            pe.wait_ge(c_taken, J + 2 + PAIRS)
                            pe.wait_ge(y_taken, J + 2 + PAIRS)
                    if start and half:
                        pe.wait_ge((z_even_copied, z_odd_copied)[b], t + 1)
                    pe.matmul(bank, mh, wh, start=start, stop=False)
                    pe.matmul(bank, mh, wl, start=False, stop=False)
                    ins = pe.matmul(bank, ml, wh, start=False, stop=first is None and i == 1)
                if first is None and i == 1 and t < TT - 1:
                    ins.then_inc(rows_done, 1)
            ins.then_inc(units_done, 1)

        def last_units():
            def block(i, t):
                mh, ml = m_hi[i][:, t * P:(t + 1) * P], m_lo[i][:, t * P:(t + 1) * P]
                for b in range(2):
                    bank = psum[:, 2 * t + b, :]
                    wh, wl = w_hi[i][:, b * T:(b + 1) * T], w_lo[i][:, b * T:(b + 1) * T]
                    pe.matmul(bank, mh, wh, start=False, stop=False)
                    pe.matmul(bank, mh, wl, start=False, stop=False)
                    ins = pe.matmul(bank, ml, wh, start=False, stop=i == 1)
                if i == 1:
                    ins.then_inc(rows_done if t < TT - 1 else units_done, 1)

            for i, tiles in ((0, range(TT - 1)), (1, range(TT - 1)), (0, (TT - 1,)), (1, (TT - 1,))):
                if tiles[0] == 0:
                    pe.wait_ge(w_lo_ready, N_OUT + 2 * KO - 1 + i)
                    pe.wait_ge(m_lo_ready, 2 * KO - 1 + i)
                for t in tiles:
                    block(i, t)

        for half in range(2):
            for i in range(2):
                out_unit(half, 0, i, True)
            with pe.Fori(1, KO // 2 - 1) as kp:
                for i in range(2):
                    out_unit(half, kp, i, False)
            if half == 0:
                for i in range(2):
                    out_unit(half, KO // 2 - 1, i, None)
        last_units()

    block_cm.__exit__(None, None, None)


def constants():
    import numpy as np
    c = np.zeros((P, C_COLS), np.float32)
    c[:, C_IDENT:C_IDENT + P] = np.eye(P)
    c[:, C_IOTA:C_IOTA + T] = np.arange(T)
    for a in range(2):
        c[:, C_MASK + a] = (np.arange(P) // H) % 2 == a
        c[:, C_HALF + a] = np.arange(P) // S == a
    c[:, C_HALFPI] = math.pi / 2
    c[:, C_QUARTER] = -0.25
    return c


_INS = ("x", "norm_pre_g", "w_in", "conv_w", "conv_b", "ssm_a_re", "ssm_a_im", "ssm_log_dt", "ssm_b_re",
        "ssm_b_im", "ssm_c_re", "ssm_c_im", "ssm_d", "w_glu", "b_glu", "w_out", "norm_post_g")


def kernel(**inputs):
    import numpy as np
    import concourse.bacc as bacc
    from concourse.bass_utils import run_bass_kernel_spmd

    nc = bacc.Bacc("TRN2", target_bir_lowering=False, num_devices=1)
    arrays = {name: np.ascontiguousarray(inputs[name]) for name in _INS}
    arrays["consts"] = constants()
    aps = [nc.dram_tensor(name, a.shape, F32, kind="ExternalInput").ap() for name, a in arrays.items()]
    result = nc.dram_tensor("result", (1, T, D), F32, kind="ExternalOutput").ap()
    build(nc, *aps, result)
    return run_bass_kernel_spmd(nc, [arrays], core_ids=[0]).results[0]["result"]
```

```python
import math

import concourse.bass as bass
from concourse import mybir

F32 = mybir.dt.float32
F32R = mybir.dt.float32r
I32 = mybir.dt.int32
ALU = mybir.AluOpType
ACT = mybir.ActivationFunctionType

P = 128
T = 512
D = 2048
DC = 1024
DS = 1024
G, S, H = 64, 64, 16
WIDTH = 3
EPS = 1e-6
KT = D // P
TT = T // P
J = DC // P
Q = 4
NQ = J * Q
KS = DS // P
KO = (DC + DS) // P
UK = 8
UC = UK * P

COL_B, COL_C, COL_V, COL_Z, COL_U, COL_G = 0, DC, 2 * DC, 3 * DC, 4 * DC, 4 * DC + DS

N_LOOP = 4
PER_J = 10
N_GATE = N_LOOP + PER_J * J
PER_P = 6
PAIRS = 3
N_GLU = N_GATE + PER_P * PAIRS
N_OUT = N_GLU + 2

C_IDENT, C_IOTA, C_MASK, C_HALF, C_HALFPI, C_QUARTER, C_COLS = 0, P, P + T, P + T + 2, P + T + 4, P + T + 5, P + T + 6
V_PRE, V_CW, V_CB, V_D, V_BG = 0, KT, KT + WIDTH * J, KT + (WIDTH + 1) * J, KT + (WIDTH + 2) * J
V_ROWS = V_BG + KS

TWO_PI = 6.2831850
INV_2PI = 1.0 / (2.0 * math.pi)
ROUND = 1.5 * 2.0 ** 23
ROUND15 = 1.5 * 2.0 ** 8
PI_A = 201.0 / 32.0
PI_B = 1014.0 / 2.0 ** 19
PI_C = 2.0 * math.pi - PI_A - PI_B
LN2_A = 355.0 / 512.0
LN2_B = math.log(2.0) - LN2_A


def build(nc, x, norm_pre_g, w_in, conv_w, conv_b, ssm_a_re, ssm_a_im, ssm_log_dt, ssm_b_re,
          ssm_b_im, ssm_c_re, ssm_c_im, ssm_d, w_glu, b_glu, w_out, norm_post_g, consts, out):
    at = [16512]

    def region(nbytes):
        start = at[0]
        at[0] += nbytes
        assert at[0] <= 229344, at[0]
        return start

    def place(name, shape, dtype, start, used=0):
        size = 4
        for n in shape[1:]:
            size *= n
        return nc.alloc_sbuf_tensor_at(name, shape, dtype, offset=start + used), used + (size + 31) // 32 * 32

    def own(name, shape, dtype=F32):
        size = 4
        for n in shape[1:]:
            size *= n
        return nc.alloc_sbuf_tensor_at(name, shape, dtype, offset=region((size + 31) // 32 * 32))

    w_raw = [own(f"w_raw{s}", [P, UC]) for s in range(2)]
    w_hi = [own(f"w_hi{s}", [P, UC], F32R) for s in range(2)]
    w_lo = [own(f"w_lo{s}", [P, UC], F32R) for s in range(2)]
    const = own("const", [P, C_COLS])
    cols = own("cols", [P, V_ROWS])
    mag = own("mag", [P, NQ])
    turn_hi = own("turn_hi", [P, NQ])
    turn_lo = own("turn_lo", [P, NQ])
    stats = own("stats", [P, 6, 8])
    v_sb = own("v_sb", [P, T])
    cv = own("cv", [P, T + WIDTH - 1])
    conv = own("conv", [P, T])
    sig = [own(f"sig{s}", [P, T]) for s in range(2)]
    b_split = own("b_split", [P, 3, 2 * P], F32R)
    c_cur = own("c_cur", [P, 2, 5 * P])

    r_h = region(2 * KT * T * 4)
    h_hi, n = place("h_hi", [P, KT, T], F32R, r_h)
    h_lo, n = place("h_lo", [P, KT, T], F32R, r_h, n)
    squares, _ = place("squares", [P, D], F32, r_h, KT * T * 4)
    x_res, n = place("x_res", [P, TT, D], F32, r_h)
    z_half, n = place("z_half", [P, TT, DC], F32, r_h, n)
    g_post, n = place("g_post", [P, D], F32, r_h, n)

    r_s = region(32 * 1024)
    x_sb, n = place("x_sb", [P, TT, D], F32, r_s)
    cos, n = place("cos", [P, Q, T], F32, r_s)
    sin, n = place("sin", [P, Q, T], F32, r_s, n)
    by_cos, n = place("by_cos", [P, 2, T], F32, r_s, n)
    by_sin, n = place("by_sin", [P, 2, T], F32, r_s, n)
    state = [None, None]
    state[0], n = place("state0", [P, 2, T], F32, r_s, n)
    state[1], n = place("state1", [P, 2, T], F32, r_s, n)
    assert n == 32 * 1024
    y_hi, n = place("y_hi", [P, KS, T], F32R, r_s)
    y_lo, n = place("y_lo", [P, KS, T], F32R, r_s, n)

    r_m = region(16 * 1024)
    b_all, n = place("b_all", [P, J, 2, P], F32, r_m)
    c_all, n = place("c_all", [P, 2, J, P], F32, r_m, n)
    glu = [None, None]
    glu[0], n = place("glu0", [P, T], F32, r_m)
    glu[1], n = place("glu1", [P, T], F32, r_m, n)
    m_hi, m_lo = [None, None], [None, None]
    for s in range(2):
        m_hi[s], n = place(f"m_hi{s}", [P, T], F32R, r_m, n)
        m_lo[s], n = place(f"m_lo{s}", [P, T], F32R, r_m, n)

    r_y = region(48 * 1024)
    y, n = place("y", [P, J, T], F32, r_y)
    mix, n = place("mix", [P, KO, T], F32, r_y, n)
    vec_rows, n = place("vec_rows", [V_ROWS, P], F32, r_y)
    par_rows, n = place("par_rows", [3 * NQ, P], F32, r_y, n)
    log_dt, n = place("log_dt", [P, 2], F32, r_y, n)
    par, n = place("par", [P, 24, NQ], F32, r_y, n)
    c_nat, n = place("c_nat", [P, 2, J, S], F32, r_y, n)
    c_pad, n = place("c_pad", [P, 2, J, 2, S], F32, r_y, n)
    b_pad, n = place("b_pad", [P, 2, NQ, 2, H], F32, r_y, n)
    b_mix, n = place("b_mix", [P, 2, NQ, H], F32, r_y, n)
    b_tmp, n = place("b_tmp", [P, 2, NQ, H], F32, r_y, n)
    b_nat, n = place("b_nat", [P, 2, NQ, H], F32, r_y, n)
    assert n <= (J + J) * T * 4 + Q * T * 4, n
    u_stack, n = place("u_stack", [P, Q, T], F32R, r_y, (J + J) * T * 4)
    u_split, n = place("u_split", [P, 2, T], F32R, r_y, n)
    b_cur, n = place("b_cur", [P, Q, 2 * P], F32R, r_y, n)
    assert n == 48 * 1024
    exp2n, _ = place("exp2n", [P, NQ], I32, r_m)

    psum = nc.alloc_psum_tensor("psum", [P, 8, T], F32)
    bank_a, bank_b, bank_c, bank_y = 4, 5, 6, 7

    ident = const[:, C_IDENT:C_IDENT + P]
    iota = const[:, C_IOTA:C_IOTA + T]
    halfpi = const[:, C_HALFPI:C_HALFPI + 1]
    minus_quarter = const[:, C_QUARTER:C_QUARTER + 1]

    z_last, n = place("z_last", [P, TT, DC], F32, r_s)
    z_root, n = place("z_root", [P, 2, DC], F32, r_s, n)
    z_sum, n = place("z_sum", [P, TT, 4], F32, r_s, n)
    last_scratch, n = place("last_scratch", [P, T], F32, r_s, n)

    sem = nc.alloc_semaphore
    const_in, rows_in, res_in = sem("const_in"), sem("rows_in"), sem("res_in")
    par_in, b_in, c_in = sem("par_in"), sem("b_in"), sem("c_in")
    gain_in = sem("gain_in")
    x_in = [sem(f"x_in{i}") for i in range(TT)]
    w_loaded = [sem(f"w_loaded{s}") for s in range(2)]
    w_hi_ready, w_lo_ready, units_done = sem("w_hi_ready"), sem("w_lo_ready"), sem("units_done")
    dve_step = sem("dve_step")
    rows_turned, par_turned, dt_spread = sem("rows_turned"), sem("par_turned"), sem("dt_spread")
    c_padded, c_turned, c_stored = sem("c_padded"), sem("c_turned"), sem("c_stored")
    b_mixed, b_padded = sem("b_mixed"), sem("b_padded")
    b_turned, b_stored = sem("b_turned"), sem("b_stored")
    cols_known = sem("cols_known")
    turns_known, lam_trig = sem("turns_known"), sem("lam_trig")
    last_x_scaled = sem("last_x_scaled")
    squared, mean_ready, root_ready = sem("squared"), sem("mean_ready"), sem("root_ready")
    x_rstd, x_scaled = sem("x_rstd"), sem("x_scaled")
    x_turned, h_hi_ready, h_ready = sem("x_turned"), sem("h_hi_ready"), sem("h_ready")
    bu_ready, bu_free = sem("bu_ready"), sem("bu_free")
    rotated, scanned, unrotated = sem("rotated"), sem("scanned"), sem("unrotated")
    state_ready, state_free = sem("state_ready"), sem("state_free")
    turn_steps, phase_ready = sem("turn_steps"), sem("phase_ready")
    trig_steps, trig_ready = sem("trig_steps"), sem("trig_ready")
    c_cur_ready = sem("c_cur_ready")
    a_taken, b_taken, c_taken, y_taken = sem("a_taken"), sem("b_taken"), sem("c_taken"), sem("y_taken")
    tap_done = sem("tap_done")
    u_hi_ready, u_lo_ready = sem("u_hi_ready"), sem("u_lo_ready")
    b_hi_ready, b_split_ready = sem("b_hi_ready"), sem("b_split_ready")
    u_stacked = [sem(f"u_stacked{pairs}") for pairs in range(2)]
    b_stacked = [sem(f"b_stacked{pairs}") for pairs in range(2)]
    sig_ready, mix_ready = sem("sig_ready"), sem("mix_ready")
    gate_sig, gelu_done, y_hi_ready, y_lo_ready = sem("gate_sig"), sem("gelu_done"), sem("y_hi_ready"), sem("y_lo_ready")
    glu_sig, glu_mul, mix_gated = sem("glu_sig"), sem("glu_mul"), sem("mix_gated")
    m_hi_ready, m_lo_ready = sem("m_hi_ready"), sem("m_lo_ready")
    rows_done, z_even_copied, z_odd_copied = sem("rows_done"), sem("z_even_copied"), sem("z_odd_copied")
    z_squared, z_gained = sem("z_squared"), sem("z_gained")
    last_gained, last_squared = sem("last_gained"), sem("last_squared")
    out_mean, out_root, rstd_known, z_scaled = sem("out_mean"), sem("out_root"), sem("rstd_known"), sem("z_scaled")
    last_left_ready = sem("last_left_ready")
    left_ready, right_ready, out_stored = sem("left_ready"), sem("right_ready"), sem("out_stored")

    w_in_units = w_in.rearrange("(u k p) c -> u p k c", k=UK, p=P)
    w_glu_units = w_glu.rearrange("(k p) c -> p k c", p=P)
    w_out_units = w_out.rearrange("(k p) c -> k p c", p=P)

    def slot(n):
        return n % 2

    def rows_finished(engine, half, t):
        if t < TT - 1:
            engine.wait_ge(rows_done, (TT - 1) * half + t + 1)
        elif half == 0:
            engine.wait_ge(units_done, N_OUT + KO)
        else:
            engine.wait_ge(units_done, N_OUT + 2 * KO - 1)

    block_cm = nc.Block()
    block = block_cm.__enter__()

    @block.sync
    def _(sp):
        sp.dma_start(log_dt[2 * NQ:3 * NQ, :], ssm_log_dt.rearrange("(q a) -> q a", a=2)).then_inc(par_in, 16)
        sp.dma_start(par_rows[0:NQ, :], ssm_a_re.rearrange("(q a) p -> q (a p)", a=2)).then_inc(par_in, 16)
        for i in range(TT):
            sp.dma_start(x_sb[:, i, :], x[0, i * P:(i + 1) * P, :]).then_inc(x_in[i], 16)

        def load(base, i, src):
            if not (isinstance(base, int) and base + i < 2):
                sp.wait_ge(w_lo_ready, base + i - 1)
            dst = w_raw[slot(i)][:, :]
            if len(src.shape) == 3:
                dst = dst.rearrange("p (k c) -> p k c", k=UK)
            sp.dma_start(dst, src).then_inc(w_loaded[slot(i)], 16)

        def tile_pair(base, i, col):
            for half in range(2):
                load(base, i + half, w_in_units[half, :, :, bass.ds(col, P)])

        def load_half(base, i, col):
            load(base, i, w_in_units[i % 2, :, :, bass.ds(col, P)])

        def stack(dst, src, again, pairs, stacked):
            for q in range(2 * pairs, 2 * pairs + 2):
                rows = src[2 * H * q:2 * H * (q + 1), :, :].bitcast(F32)
                for half, part in enumerate((0, again)):
                    sp.dma_start(dst[half * P // 2:(half + 1) * P // 2, q, :].bitcast(F32),
                                 rows[:, part:part + 2, :]).then_inc(stacked[pairs], 16)

        def channel_tile(j1, last):
            base = N_LOOP - PER_J + PER_J * j1
            tile_pair(base, 2, P * j1 + (COL_B - P))
            tile_pair(base, 4, P * j1 + (COL_Z - P))
            tile_pair(base, 6, COL_G if last else P * j1 + COL_U)
            load_half(base, 8, COL_G + P if last else P * j1 + COL_V)
            if last:
                load_half(base, 9, COL_G + P)
                return
            sp.wait_ge(b_split_ready, j1 + 1)
            stack(b_cur, b_split, 1, 0, b_stacked)
            load_half(base, 9, P * j1 + COL_V)
            stack(b_cur, b_split, 1, 1, b_stacked)
            load_half(base, PER_J, P * j1 + COL_C)
            sp.wait_ge(u_lo_ready, j1 + 1)
            stack(u_stack, u_split, 0, 0, u_stacked)
            load_half(base, PER_J + 1, P * j1 + COL_C)
            stack(u_stack, u_split, 0, 1, u_stacked)

        tile_pair(0, 0, COL_U)
        for c, src in enumerate((ssm_c_re, ssm_c_im)):
            sp.dma_start(c_nat[:, c, :, :], src.rearrange("(j g) h p -> (g h) j p", g=2 * Q)).then_inc(c_in, 16)
        for c, src in enumerate((ssm_b_re, ssm_b_im)):
            sp.dma_start(b_nat[:, c, :, :], src.rearrange("(q a) p h -> (a p) q h", a=2)).then_inc(b_in, 16)
        tile_pair(0, 2, COL_V)
        load_half(N_LOOP, 0, COL_C)
        sp.wait_ge(u_lo_ready, 1)
        for pairs in range(2):
            stack(u_stack, u_split, 0, pairs, u_stacked)
        load_half(N_LOOP, 1, COL_C)
        sp.wait_ge(b_split_ready, 1)
        for pairs in range(2):
            stack(b_cur, b_split, 1, pairs, b_stacked)
        with sp.Fori(1, J) as j1:
            channel_tile(j1, False)
        channel_tile(J, True)
        with sp.Fori(1, PAIRS + 1) as p1:
            base = N_GATE - PER_P + PER_P * p1
            tile_pair(base, 0, 2 * P * p1 + COL_G)
            tile_pair(base, 2, 2 * P * p1 + COL_G + P)
            load(base, 4, w_glu_units[:, :, bass.ds(2 * P * p1 - 2 * P, P)])
            load(base, 5, w_glu_units[:, :, bass.ds(2 * P * p1 - P, P)])
        load(N_GLU, 0, w_glu_units[:, :, 6 * P:7 * P])
        load(N_GLU, 1, w_glu_units[:, :, 7 * P:8 * P])

        def out_unit(half, kp, i):
            load(N_OUT + KO * half + 2 * kp, i, w_out_units[bass.ds(2 * kp + i, 1), :, half * UC:(half + 1) * UC]
                 .rearrange("o p c -> (o p) c"))

        out_unit(0, 0, 0)
        sp.wait_ge(units_done, N_GLU - 2)
        sp.dma_start(g_post[:, :], norm_post_g.partition_broadcast(P)).then_inc(gain_in, 16)
        out_unit(0, 0, 1)
        x_cols = D // (KO // 2)
        x_tiles = x[0].rearrange("(t p) d -> p t d", p=P)
        with sp.Fori(1, KO // 2) as kp:
            for i in range(2):
                out_unit(0, kp, i)
            sp.dma_start(x_res[:, :, bass.ds(x_cols * kp, x_cols)],
                         x_tiles[:, :, bass.ds(x_cols * kp, x_cols)]).then_inc(res_in, 16)
        sp.dma_start(x_res[:, :, 0:x_cols], x_tiles[:, :, 0:x_cols]).then_inc(res_in, 16)
        with sp.Fori(0, KO // 2) as kp:
            for i in range(2):
                out_unit(1, kp, i)

        def store(t, half, ready, count):
            sp.wait_ge(ready, count)
            cols_ = slice(half * DC, (half + 1) * DC)
            sp.dma_start(out[0, t * P:(t + 1) * P, cols_], x_res[:, t, cols_]).then_inc(out_stored, 16)

        for t in range(TT - 1):
            store(t, 1, right_ready, t + 1)
            if t:
                store(t - 1, 0, left_ready, t)
        store(TT - 1, 1, right_ready, TT)
        store(TT - 2, 0, left_ready, TT - 1)
        store(TT - 1, 0, last_left_ready, 1)
        sp.wait_ge(out_stored, 2 * 16 * TT)

    @block.gpsimd
    def _(pool):
        def remainder(base, i):
            s = slot(i)
            pool.wait_ge(w_hi_ready, base + i + 1)
            pool.tensor_tensor(w_lo[s][:, :], w_raw[s][:, :], w_hi[s][:, :].bitcast(F32),
                               ALU.subtract).then_inc(w_lo_ready, 1)

        for i in range(TT - 1):
            pool.wait_ge(x_rstd, i + 1)
            pool.tensor_scalar(x_sb[:, i, :], x_sb[:, i, :], stats[:, 3, i:i + 1], 1.0, ALU.mult, ALU.mult)\
                .then_inc(x_scaled, 1)
        remainder(0, 0)
        pool.wait_ge(const_in, 16)
        pool.wait_ge(c_in, 32)
        for c in range(2):
            for a in range(2):
                step = pool.tensor_scalar(c_pad[:, c, :, a, :], c_nat[:, c, :, :],
                                          const[:, C_MASK + a:C_MASK + a + 1], 1.0, ALU.mult, ALU.mult)
        step.then_inc(c_padded, 1)

        for i in range(1, N_LOOP):
            remainder(0, i)
        with pool.Fori(0, J) as j:
            for i in range(PER_J):
                remainder(N_LOOP + PER_J * j, i)
        with pool.Fori(0, PAIRS) as p:
            for i in range(PER_P):
                remainder(N_GATE + PER_P * p, i)
        with pool.Fori(0, KO // 2 + 2) as kp:
            for i in range(2):
                remainder(N_GLU + 2 * kp, i)
        for t in range(TT):
            for i in range(2):
                remainder(N_OUT + KO + 2 + 2 * t, i)
            if t == 0:
                pool.wait_ge(gain_in, 16)
            pool.wait_ge(z_squared, t + 1)
            pool.tensor_tensor(z_half[:, t, :], z_half[:, t, :], g_post[:, 0:DC], ALU.mult).then_inc(z_gained, 1)
        with pool.Fori(KO // 2 + 2 + TT, KO + 1) as kp:
            for i in range(2):
                remainder(N_GLU + 2 * kp, i)
        pool.wait_ge(res_in, 16 * (KO // 2))
        for t in range(TT - 1):
            pool.wait_ge(z_scaled, t + 1)
            pool.tensor_tensor(x_res[:, t, 0:DC], z_root[:, t % 2, :], x_res[:, t, 0:DC], ALU.add)\
                .then_inc(left_ready, 1)

    @block.scalar
    def _(act):
        act.dma_start(const[:, :], consts).then_inc(const_in, 16)
        act.dma_start(par_rows[NQ:2 * NQ, :], ssm_a_im.rearrange("(q a) p -> q (a p)", a=2)).then_inc(par_in, 16)
        rows = ((norm_pre_g.rearrange("(a p) -> a p", p=P), V_PRE, KT),
                (conv_w.rearrange("k (a p) -> (k a) p", p=P), V_CW, WIDTH * J),
                (conv_b.rearrange("(a p) -> a p", p=P), V_CB, J),
                (ssm_d.rearrange("(a p) -> a p", p=P), V_D, J),
                (b_glu.rearrange("(a p) -> a p", p=P), V_BG, KS))
        for src, row, count in rows:
            act.dma_start(vec_rows[row:row + count, :], src).then_inc(rows_in, 16)

        def rounded(base, i):
            s = slot(i)
            act.wait_ge(w_loaded[s], 8 * base + 16 * (i // 2 + 1))
            if not (isinstance(base, int) and base + i < 2):
                act.wait_ge(units_done, base + i - 1)
            act.activation(w_hi[s][:, :], w_raw[s][:, :], ACT.Copy).then_inc(w_hi_ready, 1)

        act.wait_ge(const_in, 16)
        act.activation(stats[:, 5, 5:6], ident[:, 0:1], ACT.Sqrt)
        for i in range(TT):
            act.wait_ge(x_in[i], 16)
            if i:
                act.wait_ge(squared, i)
            act.activation(squares[:, :], x_sb[:, i, :], ACT.Square,
                           accum_out=stats[:, 0, i:i + 1]).then_inc(squared, 1)
            for k in ((), (0, 1), (2,), (3,))[i]:
                act.wait_ge(mean_ready, k + 1)
                act.activation(stats[:, 2, k:k + 1], stats[:, 1, k:k + 1], ACT.Sqrt).then_inc(root_ready, 1)
        rounded(0, 0)
        act.wait_ge(cols_known, 1)
        for k in range(KT):
            act.wait_ge(x_turned, k + 1)
            act.activation(h_hi[:, k, :], psum[:, k % 4, :], ACT.Copy,
                           scale=cols[:, V_PRE + k:V_PRE + k + 1]).then_inc(h_hi_ready, 1)
            if k == 1:
                act.wait_ge(turns_known, 1)
                act.activation(par[:, 12, :], par[:, 11, :], ACT.Sin, scale=TWO_PI).then_inc(lam_trig, 1)
                act.activation(par[:, 13, :], par[:, 11, :], ACT.Sin, scale=TWO_PI / 2).then_inc(lam_trig, 1)
            elif k == 3:
                rounded(0, 1)
        rounded(0, 2)

        def cosines(j, q):
            act.wait_ge(phase_ready, Q * j + q + 1)
            act.activation(sin[:, q, :], cos[:, q, :], ACT.Abs, bias=minus_quarter).then_inc(trig_steps, 1)
            act.wait_ge(trig_steps, 3 * (Q * j + q) + 1)
            act.activation(cos[:, q, :], cos[:, q, :], ACT.Abs).then_inc(trig_steps, 1)
            act.activation(sin[:, q, :], sin[:, q, :], ACT.Sin, scale=-TWO_PI, bias=halfpi).then_inc(trig_steps, 1)
            act.wait_ge(trig_steps, 3 * (Q * j + q) + 2)
            act.activation(cos[:, q, :], cos[:, q, :], ACT.Sin, scale=-TWO_PI, bias=halfpi).then_inc(trig_ready, 1)

        def round_u():
            act.activation(u_split[:, 0, :], psum[:, bank_a, :], ACT.Copy).then_inc(u_hi_ready, 1)

        def copy_v():
            act.activation(v_sb[:, :], psum[:, bank_b, :], ACT.Copy).then_inc(b_taken, 1)

        act.wait_ge(units_done, 2)
        round_u()
        rounded(0, 3)

        def output_matrices(c):
            for half, bank in enumerate((bank_c, bank_y)):
                act.wait_ge(c_turned, 2 * c + half + 1)
                act.activation(c_all[:, c, 4 * half:4 * half + 4, :],
                               psum[:, bank, :].rearrange("p (j m) -> p j m", m=P),
                               ACT.Copy, scale=1.0 - 2.0 * c).then_inc(c_stored, 1)

        output_matrices(0)
        for bank in range(4):
            act.wait_ge(b_turned, bank + 1)
            act.activation(b_all[:, 2 * bank:2 * bank + 2, :, :],
                           psum[:, bank, :].rearrange("p (j c m) -> p j c m", j=2, c=2),
                           ACT.Copy).then_inc(b_stored, 1)
        output_matrices(1)
        rounded(N_LOOP, 0)
        cosines(0, 0)
        cosines(0, 1)
        act.wait_ge(units_done, N_LOOP)
        copy_v()
        rounded(N_LOOP, 1)
        cosines(0, 2)
        cosines(0, 3)

        def z_sigmoid(j):
            act.wait_ge(mix_ready, j + 1)
            act.activation(sig[0][:, :], psum[:, bank_b, :], ACT.Sigmoid).then_inc(sig_ready, 1)

        with act.Fori(0, J - 1) as j:
            base = N_LOOP + PER_J * j
            for i in range(PER_J):
                rounded(base, i + 2)
                if i == 3:
                    cosines(j + 1, 0)
                elif i == 5:
                    z_sigmoid(j)
                elif i == 6:
                    cosines(j + 1, 1)
                elif i == 7:
                    act.wait_ge(bu_ready, Q * (j + 1))
                    round_u()
                elif i == 8:
                    cosines(j + 1, 2)
                elif i == 9:
                    act.wait_ge(c_taken, j + 2)
                    copy_v()
                    cosines(j + 1, 3)
        j, base = J - 1, N_LOOP + PER_J * (J - 1)
        for i in range(PER_J):
            rounded(base, i + 2)
            if i == 5:
                z_sigmoid(j)
            elif i == 7:
                act.activation(sig[1][:, :], psum[:, bank_a, :], ACT.Sigmoid).then_inc(gate_sig, 1)
            elif i == 9:
                act.wait_ge(mix_ready, j + 2)
                act.activation(sig[0][:, :], psum[:, bank_b, :], ACT.Sigmoid).then_inc(gate_sig, 1)
        for half in range(2):
            act.wait_ge(y_taken, J + 1)
            part = y[:, 4 * half:4 * half + 4, :]
            act.activation(part, part, ACT.Gelu_apprx_tanh).then_inc(gelu_done, 1)
        with act.Fori(0, PAIRS) as p:
            base = N_GATE + PER_P * p
            for i in range(PER_P):
                rounded(base, i + 2)
                if i == 1:
                    act.wait_ge(a_taken, 2 * J + 1 + p)
                    act.activation(sig[1][:, :], psum[:, bank_a, :], ACT.Sigmoid).then_inc(gate_sig, 1)
                elif i == 3:
                    act.wait_ge(b_taken, 2 * J + 1 + p)
                    act.activation(sig[0][:, :], psum[:, bank_b, :], ACT.Sigmoid).then_inc(gate_sig, 1)
                elif i == 4:
                    act.wait_ge(c_taken, J + 2 + p)
                    act.activation(glu[0][:, :], glu[0][:, :], ACT.Sigmoid).then_inc(glu_sig, 1)
                elif i == 5:
                    act.wait_ge(y_taken, J + 2 + p)
                    act.activation(glu[1][:, :], glu[1][:, :], ACT.Sigmoid).then_inc(glu_sig, 1)
        for i, bank_sem in enumerate((c_taken, y_taken)):
            rounded(N_GLU, i + 2)
            act.wait_ge(bank_sem, J + 2 + PAIRS)
            act.activation(glu[i][:, :], glu[i][:, :], ACT.Sigmoid).then_inc(glu_sig, 1)
        with act.Fori(0, KO // 2 - 1) as kp:
            for i in range(2):
                rounded(N_OUT + 2 * kp, i + 2)
        rounded(N_OUT + KO - 2, 2)
        for t in range(TT):
            rows_finished(act, 0, t)
            act.activation(z_half[:, t, T:], psum[:, 2 * t + 1, :], ACT.Copy).then_inc(z_odd_copied, 1)
        rounded(N_OUT + KO - 2, 3)
        for t in range(TT):
            act.wait_ge(z_odd_copied, t + 1)
            act.wait_ge(z_even_copied, t + 1)
            if t >= 2:
                act.wait_ge(z_squared, t - 1)
            act.activation(z_root[:, t % 2, :], z_half[:, t, :], ACT.Square,
                           accum_out=z_sum[:, t, 0:1]).then_inc(z_squared, 1)
        with act.Fori(0, KO // 2 - 1) as kp:
            for i in range(2):
                rounded(N_OUT + KO + 2 * kp, i + 2)
        act.wait_ge(z_gained, TT)
        act.activation(stats[:, 5, 6:7], ident[:, 0:1], ACT.Sqrt)
        for pair in range(2):
            both = slice(2 * pair, 2 * pair + 2)
            for t in (2 * pair, 2 * pair + 1):
                rows_finished(act, 1, t)
                for b in range(2):
                    if b:
                        act.wait_ge(last_gained, 2 * t + 1)
                    if t or b:
                        act.wait_ge(last_squared, 2 * t + b)
                    act.activation(last_scratch[:, :], psum[:, 2 * t + 1 - b, :], ACT.Square,
                                   accum_out=z_sum[:, t, 1 + b:2 + b]).then_inc(last_squared, 1)
            act.wait_ge(out_mean, pair + 1)
            act.activation(stats[:, 4, both], stats[:, 3, both], ACT.Sqrt).then_inc(out_root, 1)
            act.wait_ge(rstd_known, pair + 1)
            for t in (2 * pair, 2 * pair + 1):
                if t == TT - 1:
                    continue
                if t >= 2:
                    act.wait_ge(left_ready, t - 1)
                else:
                    act.wait_ge(z_squared, TT)
                act.activation(z_root[:, t % 2, :], z_half[:, t, :], ACT.Copy,
                               scale=stats[:, 1, t:t + 1]).then_inc(z_scaled, 1)

    @block.vector
    def _(dve):
        steps = [0]

        def link(ins):
            steps[0] += 1
            ins.then_inc(dve_step, 1)
            dve.wait_ge(dve_step, steps[0])

        def ts(out_, in_, s1, op0, s2=None, op1=None):
            if op1 is None:
                return dve.tensor_scalar(out_, in_, s1, None, op0)
            return dve.tensor_scalar(out_, in_, s1, s2, op0, op1)

        def stt(out_, in0, scalar, op0, in1, op1):
            return dve.scalar_tensor_tensor(out=out_, in0=in0, scalar=scalar, in1=in1, op0=op0, op1=op1)

        tt = dve.tensor_tensor
        mult, add, sub = ALU.mult, ALU.add, ALU.subtract

        dve.memset(cv[:, 0:WIDTH - 1], 0.0).then_inc(mix_ready, 1)
        link(dve.memset(c_cur[:, :, :], 0.0))
        dve.wait_ge(par_in, 3 * 16)
        dve.tensor_copy(par_rows[2 * NQ:3 * NQ, :].rearrange("q (a p) -> q a p", a=2),
                        log_dt[2 * NQ:3 * NQ, :].unsqueeze(2).to_broadcast([NQ, 2, S])).then_inc(dt_spread, 1)
        dve.wait_ge(par_turned, 1)
        dve.tensor_copy(par[:, 0:3, :], psum[:, bank_y, 0:3 * NQ].rearrange("p (a q) -> p a q", a=3)).then_inc(y_taken, 1)
        dve.wait_ge(y_taken, 1)
        v = [par[:, i, :] for i in range(24)]
        (a_re, a_im, ldt, dt, arg, n, r, acc, two_n, expm1, th, turns, sin_th, sin_half, cosm1, cos_th,
         nr, ni, den, qr, qi, t0, t1, t2) = v

        def reduce_argument(x_):
            link(ts(arg, x_, -88.0, ALU.max, 89.0, ALU.min))
            link(ts(n, arg, 1.0 / math.log(2.0), mult, ROUND, add))
            link(ts(n, n, -ROUND, add, 127.0, ALU.min))
            link(stt(r, n, -LN2_A, mult, arg, add))
            link(stt(r, n, -LN2_B, mult, r, add))

        def polynomial():
            link(ts(acc, r, 1.0 / math.factorial(9), mult))
            for k in range(8, 0, -1):
                link(stt(acc, acc, 1.0 / math.factorial(k), add, r, mult))

        def exponential(out_, minus_one=None):
            link(ts(exp2n[:, :], n, 127.0, add, 2.0 ** 23, mult))
            two = exp2n[:, :].bitcast(F32)
            link(stt(out_, acc, 1.0, add, two, mult))
            if minus_one is not None:
                link(ts(two_n, two, -1.0, add))
                link(tt(t0, acc, two, mult))
                link(tt(minus_one, t0, two_n, add))

        def inverse_root(mean, root, inverse, known):
            link(dve.reciprocal(inverse, root))
            link(ts(stats[:, 5, 0:1], inverse, inverse, mult, mean, mult))
            link(ts(stats[:, 5, 1:2], stats[:, 5, 0:1], -0.5, mult, 1.5, add))
            tt(inverse, inverse, stats[:, 5, 1:2], mult).then_inc(known, 1)

        def x_norm(i):
            dve.wait_ge(squared, i + 1)
            ts(stats[:, 1, i:i + 1], stats[:, 0, i:i + 1], 1.0 / D, mult, EPS, add).then_inc(mean_ready, 1)
            dve.wait_ge(root_ready, i + 1)
            if i:
                dve.wait_ge(x_rstd, i)
            inverse_root(stats[:, 1, i:i + 1], stats[:, 2, i:i + 1], stats[:, 3, i:i + 1], x_rstd)

        reduce_argument(ldt)
        polynomial()
        exponential(dt)
        link(tt(th, a_im, dt, mult))
        link(ts(n, th, INV_2PI, mult, ROUND, add))
        link(ts(n, n, -ROUND, add))
        link(stt(r, n, -PI_A, mult, th, add))
        link(stt(r, n, -PI_B, mult, r, add))
        link(stt(r, n, -PI_C, mult, r, add))
        link(ts(turns, r, INV_2PI, mult))
        link(ts(turns, turns, 0.5, ALU.min, -0.5, ALU.max))
        dve.tensor_scalar(turn_hi[:, :], turns, ROUND15, -ROUND15, add, add).then_inc(turns_known, 1)
        dve.wait_ge(turns_known, 1)
        link(tt(turn_lo[:, :], turns, turn_hi[:, :], sub))
        link(tt(t1, a_re, dt, mult))
        reduce_argument(t1)
        x_norm(0)
        x_norm(1)
        x_norm(2)
        polynomial()
        x_norm(3)
        dve.wait_ge(x_rstd, TT)
        ts(x_sb[:, TT - 1, :], x_sb[:, TT - 1, :], stats[:, 3, TT - 1:TT], mult).then_inc(last_x_scaled, 1)
        dve.wait_ge(rows_turned, 1)
        dve.tensor_copy(cols[:, :], psum[:, bank_c, 0:V_ROWS]).then_inc(c_taken, 1)
        dve.wait_ge(c_taken, 1)
        dve.memset(stats[:, 5, 4:5], 0.0).then_inc(cols_known, 1)
        exponential(mag[:, :], expm1)

        def h_rest(k):
            dve.wait_ge(h_hi_ready, k + 1)
            stt(h_lo[:, k, :], psum[:, k % 4, :], cols[:, V_PRE + k:V_PRE + k + 1], mult,
                h_hi[:, k, :].bitcast(F32), sub).then_inc(h_ready, 1)

        h_rest(0)
        link(tt(t1, a_im, a_im, mult))
        link(tt(den, a_re, a_re, mult))
        h_rest(1)
        link(tt(den, den, t1, add))
        link(dve.reciprocal(den, den))
        h_rest(2)
        dve.wait_ge(lam_trig, 2)
        link(stt(cosm1, sin_half, -2.0, mult, sin_half, mult))
        link(ts(cos_th, cosm1, 1.0, add))
        h_rest(3)
        link(tt(t0, expm1, cos_th, mult))
        link(tt(nr, t0, cosm1, add))
        h_rest(4)
        link(tt(ni, mag[:, :], sin_th, mult))
        h_rest(5)
        link(tt(t0, nr, a_re, mult))
        link(tt(t1, ni, a_im, mult))
        h_rest(6)
        link(tt(qr, t0, t1, add))
        link(tt(qr, qr, den, mult))
        h_rest(7)
        link(tt(t0, ni, a_re, mult))
        link(tt(t1, nr, a_im, mult))
        h_rest(8)
        link(tt(qi, t0, t1, sub))
        link(tt(qi, qi, den, mult))
        for k in range(9, KT):
            h_rest(k)

        dve.wait_ge(b_in, 32)

        def over_h(a):
            return a.unsqueeze(2).to_broadcast([P, NQ, H])

        for c in range(2):
            if c:
                dve.wait_ge(b_mixed, 1)
            tt(b_tmp[:, 0, :, :], b_nat[:, c, :, :], over_h(qr), mult)
            link(tt(b_tmp[:, 1, :, :], b_nat[:, 1 - c, :, :], over_h(qi), mult))
            tt(b_mix[:, c, :, :], b_tmp[:, 0, :, :], b_tmp[:, 1, :, :], add if c else sub).then_inc(b_mixed, 1)
        for c in range(2):
            dve.wait_ge(b_mixed, c + 1)
            for a in range(2):
                ts(b_pad[:, c, :, a, :], b_mix[:, c, :, :], const[:, C_HALF + a:C_HALF + a + 1], mult)\
                    .then_inc(b_padded, 1)

        def phases(j, q):
            at_ = Q * j + q
            hi = turn_hi[:, bass.ds(at_, 1)]
            lo = turn_lo[:, bass.ds(at_, 1)]
            ts(sin[:, q, :], iota, hi, mult, -0.125, add).then_inc(turn_steps, 1)
            dve.wait_ge(turn_steps, 3 * at_ + 1)
            ts(sin[:, q, :], sin[:, q, :], ROUND, add, -ROUND, add).then_inc(turn_steps, 1)
            dve.wait_ge(turn_steps, 3 * at_ + 2)
            stt(cos[:, q, :], iota, hi, mult, sin[:, q, :], sub).then_inc(turn_steps, 1)
            dve.wait_ge(turn_steps, 3 * at_ + 3)
            stt(cos[:, q, :], iota, lo, mult, cos[:, q, :], add).then_inc(phase_ready, 1)

        def input_matrix(j):
            src = b_all[:, bass.ds(j, 1), :, :].rearrange("p o c m -> p (o c m)")
            ts(b_split[:, 2, :], src, 1.0, mult).then_inc(b_hi_ready, 1)
            ts(b_split[:, 0, :], src, 1.0, mult).then_inc(b_hi_ready, 1)
            dve.wait_ge(b_hi_ready, 2 * j + 2)
            tt(b_split[:, 1, :], src, b_split[:, 0, :].bitcast(F32), sub).then_inc(b_split_ready, 1)

        def output_matrix(j):
            dst = c_cur[:, :, :].rearrange("p c (q r) -> p c q r", r=P + 2 * H)[:, :, :, 0:2 * H]
            src = c_all[:, :, bass.ds(j, 1), :].rearrange("p c o (q r) -> p (c o) q r", r=2 * H)
            ts(dst, src, 1.0, mult).then_inc(c_cur_ready, 1)

        def skip(j):
            dve.wait_ge(u_hi_ready, j + 1)
            tt(u_split[:, 1, :], psum[:, bank_a, :], u_split[:, 0, :].bitcast(F32), sub).then_inc(u_lo_ready, 1)
            ts(y[:, bass.ds(j, 1), :].rearrange("p o t -> p (o t)"), psum[:, bank_a, :],
               cols[:, bass.ds(V_D + j, 1)], mult).then_inc(a_taken, 1)

        def over_parts(tab, q):
            return tab[:, q, :].unsqueeze(1).to_broadcast([P, 2, T])

        def scan(j, q):
            at_ = Q * j + q
            bu = psum[:, 2 * (q % 2):2 * (q % 2) + 2, :]
            st = state[q % 2]
            dve.wait_ge(bu_ready, at_ + 1)
            dve.wait_ge(trig_ready, at_ + 1)
            if q:
                dve.wait_ge(state_ready, at_)
            else:
                dve.wait_ge(c_cur_ready, j + 1)
            tt(by_cos[:, :, :], bu, over_parts(cos, q), mult)
            tt(by_sin[:, :, :], bu, over_parts(sin, q), mult).then_inc(bu_free, 1)
            dve.wait_ge(bu_free, at_ + 3)
            dve.wait_ge(state_free, at_ + 1)
            tt(st[:, 0, :], by_cos[:, 0, :], by_sin[:, 1, :], add).then_inc(rotated, 1)
            tt(st[:, 1, :], by_cos[:, 1, :], by_sin[:, 0, :], sub).then_inc(rotated, 1)
            size = mag[:, bass.ds(at_, 1)].to_broadcast([P, T])
            for c in range(2):
                dve.wait_ge(rotated, 2 * at_ + 1 + c)
                dve.tensor_tensor_scan(st[:, c, :], size, st[:, c, :], 0.0, mult, add).then_inc(scanned, 1)
            dve.wait_ge(scanned, 2 * at_ + 2)
            tt(by_cos[:, :, :], st[:, :, :], over_parts(cos, q), mult)
            tt(by_sin[:, :, :], st[:, :, :], over_parts(sin, q), mult).then_inc(unrotated, 1)
            dve.wait_ge(unrotated, at_ + 1)
            tt(st[:, 0, :], by_cos[:, 0, :], by_sin[:, 1, :], sub)
            tt(st[:, 1, :], by_cos[:, 1, :], by_sin[:, 0, :], add).then_inc(state_ready, 1)

        skip(0)
        dve.wait_ge(x_turned, KT)
        phases(0, 0)
        dve.wait_ge(b_stored, 4)
        input_matrix(0)
        dve.wait_ge(b_split_ready, 1)
        dve.memset(stats[:, 5, 2:3], 0.0).then_inc(bu_free, 2)
        for q in range(1, Q):
            phases(0, q)
        dve.wait_ge(c_stored, 4)
        output_matrix(0)

        def conv_taps(j):
            base = N_LOOP + PER_J * j
            dve.wait_ge(units_done, base + 2)
            dve.wait_ge(b_taken, 2 * j + 1)
            tt(cv[:, WIDTH - 1:], psum[:, bank_c, :], v_sb[:, :], mult).then_inc(c_taken, 1)
            dve.wait_ge(c_taken, j + 2)
            w = [cols[:, bass.ds(V_CW + J * k + j, 1)] for k in range(WIDTH)]
            ts(conv[:, :], cv[:, 0:T], w[0], mult, cols[:, bass.ds(V_CB + j, 1)], add).then_inc(tap_done, 1)
            for k in range(1, WIDTH):
                dve.wait_ge(tap_done, WIDTH * j + k)
                stt(conv[:, :], cv[:, k:k + T], w[k], mult, conv[:, :], add).then_inc(tap_done, 1)

        def gate_b(j):
            dve.wait_ge(units_done, N_LOOP + PER_J * j + 4)
            dve.wait_ge(tap_done, WIDTH * (j + 1))
            tt(conv[:, :], psum[:, bank_a, :], conv[:, :], mult).then_inc(a_taken, 1)

        def gate_z(j):
            dve.wait_ge(sig_ready, j + 1)
            dve.wait_ge(a_taken, 2 * j + 2)
            tt(conv[:, :], psum[:, bank_b, :], conv[:, :], mult).then_inc(b_taken, 1)
            dve.wait_ge(b_taken, 2 * j + 2)
            tt(mix[:, bass.ds(j, 1), :].rearrange("p o t -> p (o t)"), conv[:, :], sig[0][:, :], mult)\
                .then_inc(mix_ready, 1)

        def finish_y(j):
            dve.wait_ge(state_free, Q * (j + 1) + 2)
            dst = y[:, bass.ds(j, 1), :].rearrange("p o t -> p (o t)")
            tt(dst, psum[:, bank_y, :], dst, add).then_inc(y_taken, 1)

        def gate(m, bank, s, taken):
            dve.wait_ge(gate_sig, m + 1)
            tt(mix[:, bass.ds(J + m, 1), :].rearrange("p o t -> p (o t)"), psum[:, bank, :], sig[s][:, :], mult)\
                .then_inc(taken, 1)

        with dve.Fori(0, J - 1) as j:
            scan(j, 0)
            conv_taps(j)
            phases(j + 1, 0)
            scan(j, 1)
            gate_b(j)
            phases(j + 1, 1)
            scan(j, 2)
            gate_z(j)
            dve.wait_ge(bu_ready, Q * (j + 1))
            input_matrix(j + 1)
            scan(j, 3)
            phases(j + 1, 2)
            phases(j + 1, 3)
            skip(j + 1)
            finish_y(j)
            output_matrix(j + 1)
        j = J - 1
        scan(j, 0)
        conv_taps(j)
        scan(j, 1)
        gate_b(j)
        scan(j, 2)
        gate_z(j)
        scan(j, 3)
        gate(0, bank_a, 1, a_taken)
        gate(1, bank_b, 0, b_taken)
        finish_y(j)
        dve.wait_ge(gelu_done, 2)
        ts(y_hi[:, :, :], y[:, :, :], 1.0, mult).then_inc(y_hi_ready, 1)
        dve.wait_ge(y_hi_ready, 1)
        tt(y_lo[:, :, :], y[:, :, :], y_hi[:, :, :].bitcast(F32), sub).then_inc(y_lo_ready, 1)

        def split_mix(half, kp, i):
            at_ = KO * half + 2 * kp + i
            if isinstance(kp, int) and KO * half + kp == 0:
                dve.wait_ge(mix_ready, 1 + at_ + 1)
            else:
                dve.wait_ge(units_done, N_OUT - 1 + at_)
            src = mix[:, bass.ds(2 * kp + i, 1), :].rearrange("p o t -> p (o t)")
            ts(m_hi[i][:, :], src, 1.0, mult).then_inc(m_hi_ready, 1)
            dve.wait_ge(m_hi_ready, at_ + 1)
            tt(m_lo[i][:, :], src, m_hi[i][:, :].bitcast(F32), sub).then_inc(m_lo_ready, 1)

        for i in range(2):
            split_mix(0, 0, i)

        def glu_bias(base, m, i, bank, taken):
            dve.wait_ge(units_done, base + 5 + i)
            ts(glu[i][:, :], psum[:, bank, :], cols[:, bass.ds(V_BG + m, 1)], add).then_inc(taken, 1)

        def glu_apply(m, i):
            dve.wait_ge(glu_sig, m + 1)
            tt(glu[i][:, :], y[:, bass.ds(m, 1), :].rearrange("p o t -> p (o t)"), glu[i][:, :], mult)\
                .then_inc(glu_mul, 1)
            dve.wait_ge(glu_mul, m + 1)
            dst = mix[:, bass.ds(J + m, 1), :].rearrange("p o t -> p (o t)")
            tt(dst, dst, glu[i][:, :], mult).then_inc(mix_gated, 1)

        with dve.Fori(0, PAIRS) as p:
            base = N_GATE + PER_P * p
            gate(2 * p + 2, bank_a, 1, a_taken)
            gate(2 * p + 3, bank_b, 0, b_taken)
            glu_bias(base, 2 * p, 0, bank_c, c_taken)
            glu_apply(2 * p, 0)
            glu_bias(base, 2 * p + 1, 1, bank_y, y_taken)
            glu_apply(2 * p + 1, 1)
        glu_bias(N_GLU - 4, 6, 0, bank_c, c_taken)
        glu_apply(6, 0)
        glu_bias(N_GLU - 4, 7, 1, bank_y, y_taken)
        glu_apply(7, 1)

        dve.wait_ge(mix_gated, J)
        with dve.Fori(1, KO // 2) as kp:
            for i in range(2):
                split_mix(0, kp, i)
        split_mix(1, 0, 0)
        for t in range(TT):
            rows_finished(dve, 0, t)
            ts(z_half[:, t, 0:T], psum[:, 2 * t, :], 1.0, mult).then_inc(z_even_copied, 1)
        split_mix(1, 0, 1)
        with dve.Fori(1, KO // 2) as kp:
            for i in range(2):
                split_mix(1, kp, i)
        dve.wait_ge(z_squared, TT)
        for t in range(TT):
            link(ts(stats[:, 2, t:t + 1], z_sum[:, t, 0:1], 1.0 / D, mult, EPS, add))
        dve.wait_ge(gain_in, 16)
        dve.wait_ge(res_in, 16 * (KO // 2))
        for pair in range(2):
            both = slice(2 * pair, 2 * pair + 2)
            for t in (2 * pair, 2 * pair + 1):
                rows_finished(dve, 1, t)
                for b in range(2):
                    if b:
                        dve.wait_ge(last_squared, 2 * t + 1)
                    tt(z_last[:, t, b * T:(b + 1) * T], psum[:, 2 * t + b, :],
                       g_post[:, DC + b * T:DC + (b + 1) * T], mult).then_inc(last_gained, 1)
            dve.wait_ge(last_squared, 4 * pair + 4)
            sums = [z_sum[:, both, i:i + 1].rearrange("p t o -> p (t o)") for i in (1, 2)]
            mean, root, rstd, scratch = [stats[:, i, both] for i in (3, 4, 1, 5)]
            link(tt(mean, sums[0], sums[1], add))
            stt(mean, mean, 1.0 / D, mult, stats[:, 2, both], add).then_inc(out_mean, 1)
            dve.wait_ge(out_root, pair + 1)
            link(dve.reciprocal(rstd, root))
            link(tt(scratch, rstd, rstd, mult))
            link(tt(scratch, scratch, mean, mult))
            link(ts(scratch, scratch, -0.5, mult, 1.5, add))
            tt(rstd, rstd, scratch, mult).then_inc(rstd_known, 1)
            dve.wait_ge(rstd_known, pair + 1)
            dve.wait_ge(last_gained, 4 * pair + 4)
            for t in (2 * pair, 2 * pair + 1):
                stt(x_res[:, t, DC:], z_last[:, t, :], stats[:, 1, t:t + 1], mult, x_res[:, t, DC:], add)\
                    .then_inc(right_ready, 1)
        dve.wait_ge(z_gained, TT)
        t = TT - 1
        stt(x_res[:, t, 0:DC], z_half[:, t, :], stats[:, 1, t:t + 1], mult, x_res[:, t, 0:DC], add)\
            .then_inc(last_left_ready, 1)

    @block.tensor
    def _(pe):
        def turn(dst, src, k):
            return pe.transpose(dst, src, ident[0:k, 0:k])

        pe.wait_ge(const_in, 16)
        pe.wait_ge(dt_spread, 1)
        turn(psum[:, bank_y, 0:3 * NQ], par_rows[:, :], 3 * NQ).then_inc(par_turned, 1)

        def product(bank, k, kt, s, first, last, a_hi=h_hi, a_lo=h_lo):
            wh = w_hi[s][:, k * P:(k + 1) * P]
            wl = w_lo[s][:, k * P:(k + 1) * P]
            pe.matmul(psum[:, bank, :], wh, a_hi[:, kt, :], start=first, stop=False)
            pe.matmul(psum[:, bank, :], wh, a_lo[:, kt, :], start=False, stop=False)
            return pe.matmul(psum[:, bank, :], wl, a_hi[:, kt, :], start=False, stop=last)

        def unit(base, i, bank, half, first):
            pe.wait_ge(w_lo_ready, base + i + 1)
            for k in range(UK):
                ins = product(bank, k, UK * half + k, slot(i), first and k == 0, not first and k == UK - 1)
            ins.then_inc(units_done, 1)

        def tile(base, i, bank):
            unit(base, i, bank, 0, True)
            unit(base, i + 1, bank, 1, False)

        for t in range(TT):
            if t < TT - 1:
                pe.wait_ge(x_scaled, t + 1)
            else:
                pe.wait_ge(rows_in, 5 * 16)
                turn(psum[:, bank_c, 0:V_ROWS], vec_rows[:, :], V_ROWS).then_inc(rows_turned, 1)
                pe.wait_ge(last_x_scaled, 1)
            for k in range(4):
                ins = turn(psum[:, k, t * P:(t + 1) * P], x_sb[:, t, k * P:(k + 1) * P], P)
                if t == TT - 1:
                    ins.then_inc(x_turned, 1)
        for k in range(2, KT + 2):
            if 4 <= k < KT:
                pe.wait_ge(h_ready, k - 3)
                for t in range(TT):
                    ins = turn(psum[:, k % 4, t * P:(t + 1) * P], x_sb[:, t, k * P:(k + 1) * P], P)
                ins.then_inc(x_turned, 1)
            kt = k - 2
            if kt % UK == 0:
                pe.wait_ge(w_lo_ready, kt // UK + 1)
            pe.wait_ge(h_ready, kt + 1)
            ins = product(bank_a, kt % UK, kt, kt // UK, kt == 0, kt == KT - 1)
            if kt % UK == UK - 1:
                ins.then_inc(units_done, 1)

        def output_matrices(c):
            for half, bank in enumerate((bank_c, bank_y)):
                for j in range(4):
                    ins = turn(psum[:, bank, j * P:(j + 1) * P], c_pad[:, c, 4 * half + j, :, :], P)
                ins.then_inc(c_turned, 1)

        pe.wait_ge(c_padded, 1)
        pe.wait_ge(c_taken, 1)
        pe.wait_ge(y_taken, 1)
        output_matrices(0)
        unit(0, 2, bank_b, 0, True)
        pe.wait_ge(b_padded, 4)
        for j in range(J):
            for c in range(2):
                dst = psum[:, j // 2, ((j % 2) * 2 + c) * P:((j % 2) * 2 + c + 1) * P]
                ins = turn(dst, b_pad[:, c, Q * j:Q * j + Q, :, :], P)
                if j == 0 and c == 0:
                    ins.then_inc(state_free, 2)
                elif j % 2 and c:
                    ins.then_inc(b_turned, 1)
        pe.wait_ge(c_stored, 2)
        output_matrices(1)
        unit(0, 3, bank_b, 1, False)
        pe.wait_ge(c_stored, 4)

        def inputs(j, q):
            at_ = Q * j + q
            if q % 2 == 0:
                pe.wait_ge(b_stacked[q // 2], 16 * 4 * (j + 1))
                pe.wait_ge(u_stacked[q // 2], 16 * 4 * (j + 1))
            pe.wait_ge(bu_free, at_ + 1)
            for c in range(2):
                ins = pe.matmul(psum[:, 2 * (q % 2) + c, :], b_cur[:, q, c * P:(c + 1) * P], u_stack[:, q, :],
                                start=True, stop=True)
            ins.then_inc(bu_ready, 1)

        def outputs(j, q):
            if q == 0:
                pe.wait_ge(c_cur_ready, j + 1)
                pe.wait_ge(y_taken, j + 1)
            pe.wait_ge(state_ready, Q * j + q + 1)
            for c in range(2):
                ins = pe.matmul(psum[:, bank_y, :], c_cur[:, c, q * P:(q + 1) * P], state[q % 2][:, c, :],
                                start=(q == 0 and c == 0), stop=(q == Q - 1 and c == 1))
            ins.then_inc(state_free, 1)

        def channel_tile(j):
            base = N_LOOP + PER_J * j
            pe.wait_ge(c_taken, j + 1)
            unit(base, 0, bank_c, 0, True)
            inputs(j, 0)
            unit(base, 1, bank_c, 1, False)
            inputs(j, 1)
            pe.wait_ge(a_taken, 2 * j + 1)
            tile(base, 2, bank_a)
            inputs(j, 2)
            outputs(j, 0)
            pe.wait_ge(b_taken, 2 * j + 1)
            tile(base, 4, bank_b)
            inputs(j, 3)
            outputs(j, 1)
            pe.wait_ge(a_taken, 2 * j + 2)
            tile(base, 6, bank_a)
            outputs(j, 2)
            pe.wait_ge(b_taken, 2 * j + 2)
            tile(base, 8, bank_b)
            outputs(j, 3)

        with pe.Fori(0, J) as j:
            channel_tile(j)

        def glu_tile(base, i, bank):
            pe.wait_ge(w_lo_ready, base + i + 1)
            for k in range(KS):
                ins = product(bank, k, k, slot(i), k == 0, k == KS - 1, y_hi, y_lo)
            ins.then_inc(units_done, 1)

        with pe.Fori(0, PAIRS) as p:
            base = N_GATE + PER_P * p
            pe.wait_ge(a_taken, 2 * J + 1 + p)
            tile(base, 0, bank_a)
            pe.wait_ge(b_taken, 2 * J + 1 + p)
            tile(base, 2, bank_b)
            pe.wait_ge(y_lo_ready, 1)
            pe.wait_ge(c_taken, J + 1 + p)
            glu_tile(base, 4, bank_c)
            pe.wait_ge(y_taken, J + 1 + p)
            glu_tile(base, 5, bank_y)
        pe.wait_ge(c_taken, J + 1 + PAIRS)
        glu_tile(N_GLU, 0, bank_c)
        pe.wait_ge(y_taken, J + 1 + PAIRS)
        glu_tile(N_GLU, 1, bank_y)

        def out_unit(half, kp, i, first):
            at_ = KO * half + 2 * kp + i
            pe.wait_ge(w_lo_ready, N_OUT + at_ + 1)
            pe.wait_ge(m_lo_ready, at_ + 1)
            start = bool(first) and i == 0
            for t in range(TT):
                mh, ml = m_hi[i][:, t * P:(t + 1) * P], m_lo[i][:, t * P:(t + 1) * P]
                for b in range(2):
                    bank = psum[:, 2 * t + b, :]
                    wh, wl = w_hi[i][:, b * T:(b + 1) * T], w_lo[i][:, b * T:(b + 1) * T]
                    if start and half == 0 and t >= 2 and b == 0:
                        if t == 2:
                            pe.wait_ge(a_taken, 2 * J + 1 + PAIRS)
                            pe.wait_ge(b_taken, 2 * J + 1 + PAIRS)
                        else:
                            pe.wait_ge(c_taken, J + 2 + PAIRS)
                            pe.wait_ge(y_taken, J + 2 + PAIRS)
                    if start and half:
                        pe.wait_ge((z_even_copied, z_odd_copied)[b], t + 1)
                    pe.matmul(bank, mh, wh, start=start, stop=False)
                    pe.matmul(bank, mh, wl, start=False, stop=False)
                    ins = pe.matmul(bank, ml, wh, start=False, stop=first is None and i == 1)
                if first is None and i == 1 and t < TT - 1:
                    ins.then_inc(rows_done, 1)
            ins.then_inc(units_done, 1)

        def last_units():
            def block(i, t):
                mh, ml = m_hi[i][:, t * P:(t + 1) * P], m_lo[i][:, t * P:(t + 1) * P]
                for b in range(2):
                    bank = psum[:, 2 * t + b, :]
                    wh, wl = w_hi[i][:, b * T:(b + 1) * T], w_lo[i][:, b * T:(b + 1) * T]
                    pe.matmul(bank, mh, wh, start=False, stop=False)
                    pe.matmul(bank, mh, wl, start=False, stop=False)
                    ins = pe.matmul(bank, ml, wh, start=False, stop=i == 1)
                if i == 1:
                    ins.then_inc(rows_done if t < TT - 1 else units_done, 1)

            for i, tiles in ((0, range(TT - 1)), (1, range(TT - 1)), (0, (TT - 1,)), (1, (TT - 1,))):
                if tiles[0] == 0:
                    pe.wait_ge(w_lo_ready, N_OUT + 2 * KO - 1 + i)
                    pe.wait_ge(m_lo_ready, 2 * KO - 1 + i)
                for t in tiles:
                    block(i, t)

        for half in range(2):
            for i in range(2):
                out_unit(half, 0, i, True)
            with pe.Fori(1, KO // 2 - 1) as kp:
                for i in range(2):
                    out_unit(half, kp, i, False)
            if half == 0:
                for i in range(2):
                    out_unit(half, KO // 2 - 1, i, None)
        last_units()

    block_cm.__exit__(None, None, None)


def constants():
    import numpy as np
    c = np.zeros((P, C_COLS), np.float32)
    c[:, C_IDENT:C_IDENT + P] = np.eye(P)
    c[:, C_IOTA:C_IOTA + T] = np.arange(T)
    for a in range(2):
        c[:, C_MASK + a] = (np.arange(P) // H) % 2 == a
        c[:, C_HALF + a] = np.arange(P) // S == a
    c[:, C_HALFPI] = math.pi / 2
    c[:, C_QUARTER] = -0.25
    return c


_INS = ("x", "norm_pre_g", "w_in", "conv_w", "conv_b", "ssm_a_re", "ssm_a_im", "ssm_log_dt", "ssm_b_re",
        "ssm_b_im", "ssm_c_re", "ssm_c_im", "ssm_d", "w_glu", "b_glu", "w_out", "norm_post_g")


def kernel(**inputs):
    import numpy as np
    import concourse.bacc as bacc
    from concourse.bass_utils import run_bass_kernel_spmd

    nc = bacc.Bacc("TRN2", target_bir_lowering=False, num_devices=1)
    arrays = {name: np.ascontiguousarray(inputs[name]) for name in _INS}
    arrays["consts"] = constants()
    aps = [nc.dram_tensor(name, a.shape, F32, kind="ExternalInput").ap() for name, a in arrays.items()]
    result = nc.dram_tensor("result", (1, T, D), F32, kind="ExternalOutput").ap()
    build(nc, *aps, result)
    return run_bass_kernel_spmd(nc, [arrays], core_ids=[0]).results[0]["result"]
```
